# Optimizing a Trainium2 kernel written in Bass

```python
import jax, jax.numpy as jnp
from jax import lax
import numpy as np

D_MODEL = 2048
BATCH = 1
SEQ = 256
DEPTH = 1
DEC_BATCH = 1
DEC_SEQ = 64
PAST_LEN = 256

CHUNK = 64
D_CONV = 1024
CONV_WIDTH = 31
N_HEADS = 16
HEAD_DIM = 128
D_ATTN = N_HEADS * HEAD_DIM
IDX_HEADS = 16
IDX_DIM = 64
TOPK_MAX = 256
Q_BLOCK = 128
D_FF = -(-8 * D_MODEL // (3 * 256)) * 256
EPS = 1e-6

SPLITS = [D_CONV, D_CONV, D_ATTN, D_ATTN, D_ATTN, IDX_HEADS * IDX_DIM, IDX_DIM, IDX_HEADS, D_MODEL, D_MODEL]
D_IN = sum(SPLITS)
SPLIT_POINTS = [int(p) for p in np.cumsum(SPLITS)[:-1]]

kernel_name = "chunk_causal_conformer_dsa_hybrid_step"

def _rms_norm(x, g):
    xf = x.astype(jnp.float32)
    y = xf * lax.rsqrt(jnp.mean(xf * xf, axis=-1, keepdims=True) + EPS)
    return (y * g.astype(jnp.float32)).astype(x.dtype)

def _layer_norm(x, g, b):
    xf = x.astype(jnp.float32)
    mu = jnp.mean(xf, axis=-1, keepdims=True)
    var = jnp.mean(jnp.square(xf - mu), axis=-1, keepdims=True)
    y = (xf - mu) * lax.rsqrt(var + EPS)
    return (y * g.astype(jnp.float32) + b.astype(jnp.float32)).astype(x.dtype)

def _pre_mix(x, g_mix, w_in, idx_ln_g, idx_ln_b):
    B, T, _ = x.shape
    h = _rms_norm(x, g_mix)
    z = h @ w_in
    a, b, q, k, v, qi, ki, wi, ga, gb = jnp.split(z, SPLIT_POINTS, axis=-1)
    u = a * jax.nn.sigmoid(b)
    q = q.reshape(B, T, N_HEADS, HEAD_DIM)
    k = k.reshape(B, T, N_HEADS, HEAD_DIM)
    v = v.reshape(B, T, N_HEADS, HEAD_DIM)
    qi = qi.reshape(B, T, IDX_HEADS, IDX_DIM)
    ki = _layer_norm(ki, idx_ln_g, idx_ln_b)
    return u, q, k, v, qi, ki, wi, ga, gb

def _depthwise_causal_conv(u_padded, conv_w, conv_b):
    y = lax.conv_general_dilated(
        u_padded, conv_w[:, None, :], window_strides=(1,), padding='VALID',
        dimension_numbers=('NWC', 'WIO', 'NWC'), feature_group_count=D_CONV)
    return y + conv_b

def _sparse_attend(q, qi, wi, qpos, k, v, ki, topk):
    L = k.shape[0]
    kpos = jnp.arange(L, dtype=jnp.int32)
    limit = (qpos // CHUNK + 1) * CHUNK
    admissible = kpos[None, :] < limit[:, None]
    logits = jnp.einsum('qhd,ld->qhl', qi.astype(jnp.float32), ki.astype(jnp.float32)) * (IDX_DIM ** -0.5)
    score = jnp.einsum('qh,qhl->ql', wi.astype(jnp.float32) * (IDX_HEADS ** -0.5), jax.nn.relu(logits))
    score = jnp.where(admissible, score, -jnp.inf)
    _, sel = lax.top_k(score, topk)
    valid = jnp.take_along_axis(admissible, sel, axis=1)
    kg = k[sel]
    vg = v[sel]
    s = jnp.einsum('qhd,qkhd->qhk', q, kg, preferred_element_type=jnp.float32) * (HEAD_DIM ** -0.5)
    s = jnp.where(valid[:, None, :], s, -jnp.inf)
    p = jax.nn.softmax(s, axis=-1)
    o = jnp.einsum('qhk,qkhd->qhd', p.astype(v.dtype), vg)
    return o.reshape(q.shape[0], D_ATTN)

def _prompt_attention(q, qi, wi, k, v, ki):
    B, S = q.shape[0], q.shape[1]
    nb = S // Q_BLOCK
    topk = min(TOPK_MAX, S // 4)
    fold = lambda t: t.reshape((B * nb, Q_BLOCK) + t.shape[2:])
    b_ids = jnp.repeat(jnp.arange(B, dtype=jnp.int32), nb)
    blk_ids = jnp.tile(jnp.arange(nb, dtype=jnp.int32), B)

    def body(item):
        qb, qib, wib, bi, j = item
        qpos = j * Q_BLOCK + jnp.arange(Q_BLOCK, dtype=jnp.int32)
        return _sparse_attend(qb, qib, wib, qpos, k[bi], v[bi], ki[bi], topk)

    o = lax.map(body, (fold(q), fold(qi), fold(wi), b_ids, blk_ids))
    return o.reshape(B, S, D_ATTN)

def _sample_attention(q, qi, wi, k, v, ki, ck, cv, cki):
    P, T = ck.shape[1], q.shape[1]
    topk = min(TOPK_MAX, (P + T) // 4)
    qpos = P + jnp.arange(T, dtype=jnp.int32)

    def body(item):
        qb, qib, wib, kb, vb, kib, ckb, cvb, ckib = item
        return _sparse_attend(qb, qib, wib, qpos,
                              jnp.concatenate([ckb, kb], axis=0),
                              jnp.concatenate([cvb, vb], axis=0),
                              jnp.concatenate([ckib, kib], axis=0), topk)

    return lax.map(body, (q, qi, wi, k, v, ki, ck, cv, cki))

def _post_mix(x, conv_pre, attn_o, ga, gb, conv_ln_g, conv_ln_b, w_conv_out, w_attn_out,
              w_out, g_ffn, w_gate, w_up, w_down):
    c = jax.nn.silu(_layer_norm(conv_pre, conv_ln_g, conv_ln_b)) @ w_conv_out
    a = attn_o @ w_attn_out
    m = jax.nn.sigmoid(ga) * c + jax.nn.sigmoid(gb) * a
    x = x + m @ w_out
    h = _rms_norm(x, g_ffn)
    return x + (jax.nn.silu(h @ w_gate) * (h @ w_up)) @ w_down

def setup_inputs(seed: int = 0) -> dict:
    key = jax.random.key(seed)
    ks = jax.random.split(key, 32)
    f32 = jnp.float32
    nrm = lambda k, shape, s: jax.random.normal(k, shape, f32) * s
    return {
        'x_prompt': nrm(ks[0], (BATCH, SEQ, D_MODEL), 1.0),
        'x_sample': nrm(ks[1], (DEC_BATCH, DEC_SEQ, D_MODEL), 1.0),
        'cache_conv': nrm(ks[2], (DEPTH, DEC_BATCH, CONV_WIDTH - 1, D_CONV), 0.5),
        'cache_k': nrm(ks[3], (DEPTH, DEC_BATCH, PAST_LEN, N_HEADS, HEAD_DIM), 1.0),
        'cache_v': nrm(ks[4], (DEPTH, DEC_BATCH, PAST_LEN, N_HEADS, HEAD_DIM), 1.0),
        'cache_kidx': nrm(ks[5], (DEPTH, DEC_BATCH, PAST_LEN, IDX_DIM), 1.0),
        'g_mix': 1.0 + nrm(ks[6], (DEPTH, D_MODEL), 0.02),
        'w_in': nrm(ks[7], (DEPTH, D_MODEL, D_IN), D_MODEL ** -0.5),
        'conv_w': nrm(ks[8], (DEPTH, CONV_WIDTH, D_CONV), CONV_WIDTH ** -0.5),
        'conv_b': nrm(ks[9], (DEPTH, D_CONV), 0.01),
        'conv_ln_g': 1.0 + nrm(ks[10], (DEPTH, D_CONV), 0.02),
        'conv_ln_b': nrm(ks[11], (DEPTH, D_CONV), 0.01),
        'w_conv_out': nrm(ks[12], (DEPTH, D_CONV, D_MODEL), D_CONV ** -0.5),
        'idx_ln_g': 1.0 + nrm(ks[13], (DEPTH, IDX_DIM), 0.02),
        'idx_ln_b': nrm(ks[14], (DEPTH, IDX_DIM), 0.01),
        'w_attn_out': nrm(ks[15], (DEPTH, D_ATTN, D_MODEL), D_ATTN ** -0.5),
        'w_out': nrm(ks[16], (DEPTH, D_MODEL, D_MODEL), D_MODEL ** -0.5),
        'g_ffn': 1.0 + nrm(ks[17], (DEPTH, D_MODEL), 0.02),
        'w_gate': nrm(ks[18], (DEPTH, D_MODEL, D_FF), D_MODEL ** -0.5),
        'w_up': nrm(ks[19], (DEPTH, D_MODEL, D_FF), D_MODEL ** -0.5),
        'w_down': nrm(ks[20], (DEPTH, D_FF, D_MODEL), D_FF ** -0.5),
        'g_final': 1.0 + nrm(ks[21], (D_MODEL,), 0.02),
    }

def reference(x_prompt, x_sample, cache_conv, cache_k, cache_v, cache_kidx, g_mix, w_in, conv_w,
              conv_b, conv_ln_g, conv_ln_b, w_conv_out, idx_ln_g, idx_ln_b, w_attn_out, w_out,
              g_ffn, w_gate, w_up, w_down, g_final):
    xp, xs = x_prompt, x_sample
    conv_p, k_p, v_p, kidx_p = [], [], [], []
    conv_s, k_s, v_s, kidx_s = [], [], [], []
    for l in range(DEPTH):
        u, q, k, v, qi, ki, wi, ga, gb = _pre_mix(xp, g_mix[l], w_in[l], idx_ln_g[l], idx_ln_b[l])
        u_pad = jnp.pad(u, ((0, 0), (CONV_WIDTH - 1, 0), (0, 0)))
        conv_pre = _depthwise_causal_conv(u_pad, conv_w[l], conv_b[l])
        attn_o = _prompt_attention(q, qi, wi, k, v, ki)
        xp = _post_mix(xp, conv_pre, attn_o, ga, gb, conv_ln_g[l], conv_ln_b[l], w_conv_out[l],
                       w_attn_out[l], w_out[l], g_ffn[l], w_gate[l], w_up[l], w_down[l])
        conv_p.append(u_pad[:, -(CONV_WIDTH - 1):, :])
        k_p.append(k)
        v_p.append(v)
        kidx_p.append(ki)
        u, q, k, v, qi, ki, wi, ga, gb = _pre_mix(xs, g_mix[l], w_in[l], idx_ln_g[l], idx_ln_b[l])
        u_cat = jnp.concatenate([cache_conv[l].astype(u.dtype), u], axis=1)
        conv_pre = _depthwise_causal_conv(u_cat, conv_w[l], conv_b[l])
        attn_o = _sample_attention(q, qi, wi, k, v, ki, cache_k[l], cache_v[l], cache_kidx[l])
        xs = _post_mix(xs, conv_pre, attn_o, ga, gb, conv_ln_g[l], conv_ln_b[l], w_conv_out[l],
                       w_attn_out[l], w_out[l], g_ffn[l], w_gate[l], w_up[l], w_down[l])
        conv_s.append(u_cat[:, -(CONV_WIDTH - 1):, :])
        k_s.append(k)
        v_s.append(v)
        kidx_s.append(ki)
    y_prompt = _rms_norm(xp, g_final)
    y_sample = _rms_norm(xs, g_final)
    return (y_prompt, y_sample,
            jnp.stack(conv_p), jnp.stack(k_p), jnp.stack(v_p), jnp.stack(kidx_p),
            jnp.stack(conv_s), jnp.stack(k_s), jnp.stack(v_s), jnp.stack(kidx_s))


_drawn_inputs = setup_inputs


def setup_inputs(seed=0):
    import zlib

    import numpy as np

    out = dict(_drawn_inputs(seed))
    spreads = {}
    factors = {'conv_b': 7.544,
     'conv_ln_g': 7.059,
     'conv_ln_b': 30.105,
     'idx_ln_g': 7.847,
     'idx_ln_b': 16.452,
     'g_ffn': 3.999,
     'g_final': 7.642}
    for name, (base, spread) in spreads.items():
        noise = np.random.default_rng([zlib.crc32(name.encode()), seed]).standard_normal(out[name].shape)
        drawn = base * np.exp(spread * noise) if base else spread * noise
        out[name] = __import__('jax').numpy.asarray(drawn.astype(out[name].dtype))
    for name, factor in factors.items():
        out[name] = (out[name] * factor).astype(out[name].dtype)
    return out
```

```python
import concourse.bass as bass
from concourse import mybir
from contextlib import ExitStack


class Stream:
    SLOTS = 4

    def __init__(self, before, loops, n):
        self.n, self.loops = n, loops
        self.start = before.start + before.loops * before.n if before else 0
        self.uses0 = [before.uses0[s] + before.loops * before.per_slot(s) if before else 0
                      for s in range(self.SLOTS)]
        self.before = before

    def per_slot(self, s):
        return len(range(s, self.n, self.SLOTS))

    def count(self, i, u):
        return i * self.n + (self.start + u + 1)

    def fills(self, i, u):
        s = u % self.SLOTS
        return i * self.per_slot(s) + (self.uses0[s] + u // self.SLOTS + 1)

    def freed(self, i, u):
        if u >= self.SLOTS:
            return self.count(i, u - self.SLOTS)
        back = []
        for p in (self, self.before):
            if p is not None and p.per_slot(u):
                last = max(range(u, p.n, self.SLOTS))
                back.append(p.n - last + u)
        if self.before is None:
            return None if isinstance(i, int) and i == 0 else self.count(i, u) - back[0]
        return self.count(i, u) - min(back)


class Steps:

    def __init__(self):
        self.base, self.k, self.per, self.i, self.first = 0, 0, 0, None, 0

    def up(self):
        self.k += 1
        return self.now()

    def now(self):
        n = self.base + self.k
        return n if self.i is None else self.i * self.per + (n - self.first * self.per)

    def enter(self, i, per, first=0):
        self.i, self.per, self.first = i, per, first
        self.base, self.k = self.base + self.k, 0

    def leave(self, trips):
        assert self.k == self.per, (self.k, self.per)
        self.base, self.k, self.i = self.base + trips * self.per, 0, None


def chunk_causal_conformer_kernel(nc, a, o):
    f32, f32r = mybir.dt.float32, mybir.dt.float32r
    ALU, ACT = mybir.AluOpType, mybir.ActivationFunctionType
    ds = bass.ds

    _, TP, D = a["x_prompt"].shape
    TS = a["x_sample"].shape[1]
    T = TP + TS
    PAST, H, HD = a["cache_k"].shape[2:5]
    TAPS, DC = a["conv_w"].shape[1:3]
    PAD = TAPS - 1
    DI = a["cache_kidx"].shape[3]
    HI = 16
    DFF = a["w_gate"].shape[2]
    P = 128
    CHUNK = 64
    EPS = 1e-6
    KD, KC, KF = D // P, DC // P, DFF // P
    KFA = 32
    KFB = KF - KFA
    KU, NU = 4, 256
    SK = PAST + TS
    TOP_P, TOP_S = TP // 4, SK // 4
    assert (TP, TS, PAST, CHUNK, HD, DI) == (256, 64, 256, 64, 128, 64) and TOP_P % 8 == 0 and TOP_S % 8 == 0
    C_A, C_B, C_Q = 0, DC, 2 * DC
    C_K, C_V, C_QI = C_Q + D, C_Q + 2 * D, C_Q + 3 * D
    C_KI = C_QI + HI * DI
    C_GA = C_KI + DI + HI
    C_GB = C_GA + D
    NKI = DI + HI
    PAIRS = H // 2
    SCALE = float(HD) ** -0.5
    IDX_SCALE = float(DI) ** -0.5 * float(HI) ** -0.5
    REMOVED, OUTSIDE, IS_REMOVED, BIG = -3.0e38, -1.0e38, -2.0e38, -1.0e30
    ALL_Q = T
    CW = TP + PAD + TS
    UW = PAD + CW

    W_KI = Stream(None, 1, KD // KU)
    W_QI = Stream(W_KI, HI * DI // NU, KD // KU)
    W_CONV = Stream(W_QI, DC // NU, 2 * KD // KU)
    W_HEAD = Stream(W_CONV, PAIRS, 3 * KD // KU)
    W_MERGE = Stream(W_HEAD, D // NU, (3 * KD + KC) // KU)
    W_OUT = Stream(W_MERGE, D // NU // 2, 2 * KD // KU)
    W_UPA = Stream(W_OUT, KFA // 2, 2 * KD // KU)
    W_DNA = Stream(W_UPA, D // NU, KFA // KU)
    W_UPB = Stream(W_DNA, KFB // 2, 2 * KD // KU)
    W_DNB = Stream(W_UPB, D // NU, KFB // KU)

    ACT_EV, DVE_EV, GROUPS = {}, {}, {}
    act_n = dve_n = grp_n = 0
    for ph, per_act, per_dve, per_grp in ((W_KI, 1, 0, 0), (W_QI, 2, 0, 1), (W_CONV, 2, 2, 2), (W_HEAD, 6, 0, 3),
                                          (W_MERGE, 4, 4, 4), (W_OUT, 0, 4, 2), (W_UPA, 2, 2, 2), (W_DNA, 0, 2, 1),
                                          (W_UPB, 2, 2, 2), (W_DNB, 0, 2, 1)):
        ACT_EV[ph], DVE_EV[ph], GROUPS[ph] = (act_n, per_act), (dve_n, per_dve), (grp_n, per_grp)
        act_n += per_act * ph.loops
        dve_n += per_dve * ph.loops
        grp_n += per_grp * ph.loops

    def at(table, ph, i, k):
        base, per = table[ph]
        return i * per + (base + k)

    w_in, w_out = a["w_in"][0], a["w_out"][0]
    w_conv_out, w_attn_out = a["w_conv_out"][0], a["w_attn_out"][0]
    w_gate, w_up, w_down = a["w_gate"][0], a["w_up"][0], a["w_down"][0]

    ctx = ExitStack()
    with ctx:
        place = [(nc.sbuf_base + 31) // 32 * 32]

        def sb(name, shape, dt=f32, offset=None):
            size = 4
            for n in shape[1:]:
                size *= n
            if offset is None:
                offset = place[0]
                place[0] = (offset + size + 31) // 32 * 32
            return nc.alloc_sbuf_tensor_at(name, shape, dt, offset=offset)

        xT = sb("xT", [P, KD, T])
        at_h_hi = place[0]
        h_hi = sb("h_hi", [P, KD, T], f32r)
        at_h_lo = place[0]
        h_lo = sb("h_lo", [P, KD, T], f32r)
        w_raw = sb("w_raw", [P, 4, KU * NU])
        w_hi = sb("w_hi", [P, 4, KU * NU], f32r)
        w_lo = sb("w_lo", [P, 4, KU * NU], f32r)
        ident = sb("ident", [P, P])
        ones = sb("ones", [P, P])
        NV = 3 * KD + 3 * KC
        vecs = sb("vecs", [P, NV])
        G_MIX, G_FFN, G_FIN = vecs[:, 0:KD], vecs[:, KD:2 * KD], vecs[:, 2 * KD:3 * KD]
        CONV_B, LN_G, LN_B = (vecs[:, 3 * KD + j * KC:3 * KD + (j + 1) * KC] for j in range(3))
        conv_w = sb("conv_w_cols", [P, KC, TAPS + 1])
        idx_g = sb("idx_g", [P, DI])
        idx_b = sb("idx_b", [P, DI])
        eps = sb("eps", [P, 1])
        stat = sb("stat", [P, 8])
        bn = sb("bn", [P, 3, 6])
        mv = sb("mv", [P, 3, 2])
        istd = sb("istd", [P, 3])
        top8 = sb("top8", [P, 3, 8])
        smax = sb("smax", [P, 2, 3])
        snmax = sb("snmax", [P, 2, 3])
        ssum = sb("ssum", [P, 2, 3])
        srec = sb("srec", [P, 2, 3])
        at_cur = place[0]
        u_cur = sb("u_cur", [P, UW])
        w_cur = sb("w_cur", [P, TAPS + 1])
        acc = sb("acc", [P, CW])
        diag = sb("diag", [P, 3, P], offset=at_cur)

        A0 = place[0]
        x_tok = sb("x_tok", [P, 3, D], offset=A0)
        rows = sb("rows", [NV, P], offset=A0 + 24576)
        conv_w_rows = sb("conv_w_rows", [TAPS, DC], offset=A0 + 24576 + 512)
        cache_rows = sb("cache_rows", [PAD, DC], offset=A0 + 24576 + 512 + 4096)
        junk = sb("junk", [P, D], offset=at_h_lo)
        o_hi = sb("o_hi", [P, KD, T], f32r, offset=A0)
        o_lo = sb("o_lo", [P, KD, T], f32r, offset=A0 + 4 * KD * T)
        conv_rows_out = sb("conv_rows_out", [PAD, 2, DC], offset=A0)
        A1 = A0 + 8 * KD * T
        u_all = sb("u_all", [P, KC, UW], offset=A1)
        c_all = sb("c_all", [P, KC, T], offset=A1 + 4 * KC * UW)
        A2 = A1 + 4 * KC * (UW + T)
        place[0] = A2
        k_tok = sb("k_tok", [P, 3, NU])
        v_tok = sb("v_tok", [P, 3, NU])
        ck_tok = sb("ck_tok", [P, 2, NU])
        cv_tok = sb("cv_tok", [P, 2, NU])
        ck_T = sb("ck_T", [P, 2, PAST])
        vT = sb("vT", [P, 2, T])
        SW = P + TP + SK
        scr = [sb("scr0", [P, SW]), sb("scr1", [P, SW])]
        bias = sb("bias", [P, SW])
        PW = TP + P + 3 * TS
        pT = sb("pT", [P, PW])
        at_q = place[0]
        qT = sb("qT", [P, 2, T])
        kT = sb("kT", [P, 2, T])
        end_attention = place[0]
        hf = [sb("hf0", [P, KU, T], offset=A2), sb("hf1", [P, KU, T], offset=A2 + 4 * KU * T)]
        place[0] = A2
        kiw = sb("kiw", [P, T])
        ki_tok = sb("ki_tok", [P, 3, 2 * DI])
        kiT = sb("kiT", [P, TP + SK])
        cki_tok = sb("cki_tok", [P, 2, 2 * DI])
        w_tok = sb("w_tok", [P, 3, HI])
        w_grp = sb("w_grp", [P, 3, 4])
        sig_b = sb("sig_b", [P, 2, T], offset=A2 + 8192)
        qiT = sb("qiT", [P, 2, T], offset=A2 + 12288)
        assert place[0] <= A2 + 8192
        score = scr[0]
        relu_sc = [scr[1], bias]
        m_all = sb("m_all", [P, KD, T], offset=A1)
        c_sq = sb("c_sq", [P, KC, T], offset=A1)
        s_hi = sb("s_hi", [P, KC, T], f32r, offset=A2)
        s_lo = sb("s_lo", [P, KC, T], f32r, offset=A2 + 4 * KC * T)
        m_tmp = sb("m_tmp", [P, 2, T], offset=A2 + 8 * KC * T)
        m_tmp2 = sb("m_tmp2", [P, 2, T], offset=A2 + 8 * KC * T + 8 * T)
        s_f = [m_all[:, KD - 4:KD - 2, :], m_all[:, KD - 2:KD, :]]
        sig_a = qT
        sig_g = kT
        assert A2 + 8 * KC * T + 16 * T <= at_q
        act_hi = sb("act_hi", [P, KFA, T], f32r, offset=A0)
        act_lo = sb("act_lo", [P, KFA, T], f32r, offset=A0 + 4 * KFA * T)
        place[0] = A0 + 8 * KFA * T
        silu_g = sb("silu_g", [P, 2, T])
        act_f = sb("act_f", [P, 2, T])
        sq = sb("sq", [P, 2, T])
        ssq = sb("ssq", [P, T])
        rstd = sb("rstd", [P, T])
        end_ffn = place[0]
        rstd0 = sb("rstd0", [P, T], offset=at_cur + 1536)
        y_tok = sb("y_tok", [P, 3, D], offset=A0)
        y_c = act_f
        assert max(end_attention, end_ffn) <= nc.sbuf_usable_end, (end_attention, end_ffn, nc.sbuf_usable_end)

        M = [ctx.enter_context(nc.psum_tensor(f"M{n}", [P, 512], f32)) for n in range(4)]
        T0, T1, S0, S1 = (ctx.enter_context(nc.psum_tensor(n, [P, 512], f32)) for n in ("T0", "T1", "S0", "S1"))
        SET = [M[0:2], M[2:4]]

        def sem(name):
            return ctx.enter_context(nc.semaphore(name))

        x_in, rows_in, conv_in, idx_in = sem("x_in"), sem("rows_in"), sem("conv_in"), sem("idx_in")
        raw_full = [sem(f"raw_full{s}") for s in range(4)]
        hi_ready, lo_ready = sem("hi_ready"), sem("lo_ready")
        units_used = sem("units_used")
        first_done = sem("first_done")
        act_evac, dve_evac = sem("act_evac"), sem("dve_evac")
        consts, pads = sem("consts"), sem("pads")
        rows_T, conv_T, cache_T, x_T = sem("rows_T"), sem("conv_T"), sem("cache_T"), sem("x_T")
        vecs_ready, convw_ready, x_evac = sem("vecs_ready"), sem("convw_ready"), sem("x_evac")
        x_std, diag_ready, rstd_sum = sem("x_std"), sem("diag_ready"), sem("rstd_sum")
        hf_ready, h_hi_ready, h_ready = sem("hf_ready"), sem("h_hi_ready"), sem("h_ready")
        kiw_T, ki_var, ki_std, ki_done, kiT_done, kiT_ready = (
            sem(n) for n in ("kiw_T", "ki_var", "ki_std", "ki_done", "kiT_done", "kiT_ready"))
        idx_scored, relu_done, score_added = sem("idx_scored"), sem("relu_done"), sem("score_added")
        conv_tail_T, conv_rows_ready, conv_tail_out = (
            sem(n) for n in ("conv_tail_T", "conv_rows_ready", "conv_tail_out"))
        ck_full, cv_full, kv_out, kv_stored = (sem(n) for n in ("ck_full", "cv_full", "kv_out", "kv_stored"))
        ck_T_done, scores_done, v_T_done, k_T_done = (
            sem(n) for n in ("ck_T_done", "scores_done", "v_T_done", "k_T_done"))
        pT_done, pv_done, t_evac = sem("pT_done"), sem("pv_done"), sem("t_evac")
        scored, exp_done, rec_ready, p_ready = sem("scored"), sem("exp_done"), sem("rec_ready"), sem("p_ready")
        o_hi_done, o_lo_done = sem("o_hi_done"), sem("o_lo_done")
        conv_done, mean_done, centred, squared = sem("conv_done"), sem("mean_done"), sem("centred"), sem("squared")
        var_done, ln_std, s_scaled, s_f_ready, s_hi_ready, s_ready = (
            sem(n) for n in ("var_done", "ln_std", "s_scaled", "s_f_ready", "s_hi_ready", "s_ready"))
        x_squared, ssq_added, ssq_sum, norm_std, m_done = (
            sem(n) for n in ("x_squared", "ssq_added", "ssq_sum", "norm_std", "m_done"))
        act_hi_ready, act_lo_ready = sem("act_hi_ready"), sem("act_lo_ready")
        y_ready, y_T, y_evac, y_out = sem("y_ready"), sem("y_T"), sem("y_evac"), sem("y_out")
        dve_step, act_step, small_out = sem("dve_step"), sem("act_step"), sem("small_out")

        block = ctx.enter_context(nc.Block())

        HEAD_STEPS = ("cached keys", "scores 0", "scores 1", "values", "keys", "probs 0", "out 0", "probs 1", "out 1")

        @block.sync
        def _(sp):
            sp.dma_start(x_tok[:, 0:2, :], a["x_prompt"][0].rearrange("(t p) d -> p t d", p=P)).then_inc(x_in, 16)
            sp.dma_start(x_tok[0:TS, 2, :], a["x_sample"][0]).then_inc(x_in, 16)

            def load(ph, i, u, w, k, col, n=NU, also_next=False, waited=False):
                s = u % 4
                if ph.freed(i, u) is not None and not waited:
                    sp.wait_ge(lo_ready, ph.freed(i, u + also_next))
                dst = w_raw[:, s, 0:KU * n].rearrange("p (t n) -> p t n", n=n)
                src = w[k * P:(k + KU) * P, :].rearrange("(t p) n -> p t n", p=P)[:, :, ds(col, n)]
                sp.dma_start(dst, src).then_inc(raw_full[s], 16)

            for u in range(KD // KU):
                load(W_KI, 0, u, w_in, KU * u, C_KI, NKI)
            with sp.Fori(0, W_QI.loops) as i:
                for u in range(4):
                    load(W_QI, i, u, w_in, KU * u, i * NU + C_QI)
            with sp.Fori(1, W_CONV.loops + 1) as j:
                i = j - 1
                for u in range(8):
                    load(W_CONV, i, u, w_in, KU * (u % 4), i * NU + (C_B, C_A)[u // 4], also_next=u == 3, waited=u == 4)
            with sp.Fori(0, W_HEAD.loops) as i:
                for u in range(12):
                    load(W_HEAD, i, u, w_in, KU * (u % 4), i * NU + (C_Q, C_K, C_V)[u // 4])
            with sp.Fori(1, W_MERGE.loops + 1) as j:
                i = j - 1
                for u in range(14):
                    w, c = ((w_in, C_GA), (w_in, C_GB), (w_attn_out, 0), (w_conv_out, 0))[u // 4]
                    load(W_MERGE, i, u, w, KU * (u % 4), i * NU + c, also_next=u == 7, waited=u == 8)
            with sp.Fori(1, W_OUT.loops + 1) as j:
                i = j - 1
                for u in range(8):
                    load(W_OUT, i, u, w_out, KU * (u % 4), i * (2 * NU) + NU * (u // 4))
            for up, down, k0, nk in ((W_UPA, W_DNA, 0, KFA), (W_UPB, W_DNB, KFA, KFB)):
                with sp.Fori(1, up.loops + 1) as j:
                    i = j - 1
                    for u in range(8):
                        load(up, i, u, (w_gate, w_up)[u // 4], KU * (u % 4), i * NU + k0 * P)
                with sp.Fori(1, down.loops + 1) as j:
                    i = j - 1
                    for u in range(nk // KU):
                        load(down, i, u, w_down, k0 + KU * u, i * NU)

        @block.gpsimd
        def _(pool):
            pool.sem_inc(kv_stored, 1)
            nc.gpsimd.memset(ident[:], 0.0).then_inc(consts, 1)
            nc.gpsimd.memset(ones[:], 1.0).then_inc(consts, 1)
            nc.gpsimd.memset(eps[:], EPS).then_inc(consts, 1)
            pool.wait_ge(consts, 3)
            nc.gpsimd.affine_select(out=ident[:], in_=ident[:], compare_op=ALU.not_equal, fill=1.0, base=0,
                                    pattern=[[-1, P]], channel_multiplier=1).then_inc(consts, 1)
            at_row = 0
            for name in ("g_mix", "g_ffn", "g_final", "conv_b", "conv_ln_g", "conv_ln_b"):
                v = a[name] if name == "g_final" else a[name][0]
                v = v.rearrange("(r c) -> r c", c=P)
                pool.dma_start(rows[at_row:at_row + v.shape[0], :], v).then_inc(rows_in, 16)
                at_row += v.shape[0]
            pool.dma_start(conv_w_rows[:], a["conv_w"][0]).then_inc(conv_in, 16)
            pool.dma_start(cache_rows[:], a["cache_conv"][0, 0]).then_inc(conv_in, 16)
            pool.dma_start(idx_g[:], a["idx_ln_g"][0].partition_broadcast(P)).then_inc(idx_in, 16)
            pool.dma_start(idx_b[:], a["idx_ln_b"][0].partition_broadcast(P)).then_inc(idx_in, 16)
            nc.gpsimd.memset(u_all[:, :, 0:PAD], 0.0).then_inc(pads, 1)
            pool.wait_ge(h_ready, 4)
            cki = a["cache_kidx"][0, 0].rearrange("(t p) d -> p t d", p=P)
            pool.dma_start(cki_tok[:, :, 0:DI], cki).then_inc(idx_in, 16)
            pool.dma_start(cki_tok[:, :, DI:2 * DI], cki).then_inc(idx_in, 16)
            pool.wait_ge(ki_done, 2)
            pool.dma_start(o["kidx_p"][0, 0].rearrange("(t p) d -> p t d", p=P),
                           ki_tok[:, 0:2, 0:DI]).then_inc(small_out, 16)
            pool.dma_start(o["kidx_s"][0, 0], ki_tok[0:TS, 2, 0:DI]).then_inc(small_out, 16)

            ck_v = a["cache_k"][0, 0].rearrange("(t p) h d -> p t (h d)", p=P)
            cv_v = a["cache_v"][0, 0].rearrange("(t p) h d -> p t (h d)", p=P)
            outs = [(o["k_p"], o["k_s"], k_tok), (o["v_p"], o["v_s"], v_tok)]

            def load_cached(p):
                pool.dma_start(ck_tok[:], ck_v[:, :, ds(p * NU, NU)]).then_inc(ck_full, 16)
                pool.dma_start(cv_tok[:], cv_v[:, :, ds(p * NU, NU)]).then_inc(cv_full, 16)

            def store_kv(p):
                pool.wait_ge(t_evac, 9 * p + 5)
                for prompt, sample, tok in outs:
                    pool.dma_start(prompt[0, 0].rearrange("(t p) h d -> p t (h d)", p=P)[:, :, ds(p * NU, NU)],
                                   tok[:, 0:2, :]).then_inc(kv_out, 16)
                    pool.dma_start(sample[0, 0].rearrange("t h d -> t (h d)")[:, ds(p * NU, NU)],
                                   tok[0:TS, 2, :]).then_inc(kv_out, 16)

            pool.wait_ge(small_out, 32)
            pool.wait_ge(dve_evac, at(DVE_EV, W_HEAD, 0, 0))
            pool.wait_ge(score_added, HI + 2)
            load_cached(0)
            pool.wait_ge(conv_rows_ready, 4)
            pool.dma_start(o["conv_p"][0, 0], conv_rows_out[:, 0, :]).then_inc(conv_tail_out, 16)
            pool.dma_start(o["conv_s"][0, 0], conv_rows_out[:, 1, :]).then_inc(conv_tail_out, 16)
            with pool.Fori(0, PAIRS - 1) as p:
                store_kv(p)
                pool.wait_ge(pv_done, 2 * p + 3)
                load_cached(p + 1)
                pool.wait_ge(kv_out, 64 * p + 64)
                pool.sem_inc(kv_stored, 1)
            store_kv(PAIRS - 1)
            pool.wait_ge(kv_out, 64 * PAIRS)
            pool.sem_inc(kv_stored, 1)
            pool.wait_ge(conv_tail_out, 32)
            for q in range(4):
                pool.wait_ge(y_evac, 4 * q + 4)
                cols = slice(q * 4 * P, (q + 1) * 4 * P)
                pool.dma_start(o["y_prompt"][0].rearrange("(t p) d -> p t d", p=P)[:, :, cols],
                               y_tok[:, 0:2, cols]).then_inc(y_out, 16)
                pool.dma_start(o["y_sample"][0][:, cols], y_tok[0:TS, 2, cols]).then_inc(y_out, 16)
            pool.wait_ge(y_out, 128)

        @block.tensor
        def _(pe):
            mm, tr = nc.tensor.matmul, nc.tensor.transpose
            TOK = [(0, 0, P), (1, P, P), (2, TP, TS)]

            def unit(ph, i, u, k0, first, last, banks, hi, lo, n=NU, free=None, part=None):
                s = u % 4
                pe.wait_ge(hi_ready, ph.count(i, u))
                pe.wait_ge(lo_ready, ph.count(i, u))
                if part is not None:
                    pe.wait_ge(*part)
                tiles = [(b, b * P, min(P, n - b * P)) for b in range((n + P - 1) // P)]
                for b, c, m in tiles:
                    if first and free is not None:
                        pe.wait_ge(free[0], free[1](b))
                    for kk in range(KU):
                        wc = kk * n + c
                        start, stop = first and kk == 0, last and kk == KU - 1
                        x_hi, x_lo = hi[:, k0 + kk, :], lo[:, k0 + kk, :]
                        out = banks[b][0:m, 0:T]
                        mm(out, w_hi[:, s, wc:wc + m], x_hi, start=start, stop=False)
                        mm(out, w_hi[:, s, wc:wc + m], x_lo, start=False, stop=False)
                        done = mm(out, w_lo[:, s, wc:wc + m], x_hi, start=False, stop=stop)
                    if b == len(tiles) - 1:
                        done.then_inc(units_used, 1)
                    elif last:
                        done.then_inc(first_done, 1)

            pe.wait_ge(consts, 4)
            pe.wait_ge(rows_in, 96)
            tr(S0[:, 0:NV], rows[:], ident[0:NV, 0:NV]).then_inc(rows_T, 1)
            pe.wait_ge(conv_in, 32)
            for c in range(KC):
                done = tr(S1[:, c * TAPS:(c + 1) * TAPS], conv_w_rows[:, c * P:(c + 1) * P], ident[0:TAPS, 0:TAPS])
            done.then_inc(conv_T, 1)
            for c in range(KC):
                done = tr(T1[:, c * PAD:(c + 1) * PAD], cache_rows[:, c * P:(c + 1) * P], ident[0:PAD, 0:PAD])
            done.then_inc(cache_T, 1)
            pe.wait_ge(x_in, 32)
            for k in range(KD):
                if k >= 4:
                    pe.wait_ge(x_evac, k - 3)
                for t, c, n in TOK:
                    done = tr(M[k % 4][:, c:c + n], x_tok[0:n, t, k * P:(k + 1) * P], ident[0:n, 0:n])
                done.then_inc(x_T, 1)
            pe.wait_ge(diag_ready, 1)
            for t, c, n in TOK:
                done = mm(T0[:, c:c + n], ones[0:n, :], diag[0:n, t, 0:n], start=True, stop=True)
            done.then_inc(rstd_sum, 1)

            pe.wait_ge(x_evac, KD)
            for u in range(4):
                unit(W_KI, 0, u, KU * u, u == 0, u == 3, [M[0]], h_hi, h_lo, n=NKI, part=(h_ready, u + 1))

            def score_index_head(p, hh):
                r = slice(DI * (hh % 2), DI * (hh % 2) + DI)
                q = qiT[r, hh // 2, :]
                pe.wait_ge(relu_done, 4 * p + (hh + 1))
                mm(S0[:, 0:P], q[:, 0:P], kiT[r, 0:P], start=True, stop=True)
                mm(S0[:, P:P + TP], q[:, P:TP], kiT[r, 0:TP], start=True, stop=True)
                mm(S1[0:TS, 0:SK], q[:, TP:T], kiT[r, TP:TP + SK], start=True, stop=True).then_inc(idx_scored, 1)

            for u in range(4):
                unit(W_QI, 0, u, KU * u, u == 0, u == 3, SET[1], h_hi, h_lo)
                if u == 0:
                    pe.wait_ge(act_evac, 1)
                    for t, c, n in TOK:
                        done = tr(T0[0:n, t * NKI:(t + 1) * NKI], kiw[0:NKI, c:c + n], ident[0:NKI, 0:NKI])
                    done.then_inc(kiw_T, 1)
            pe.wait_ge(idx_in, 64)
            pe.wait_ge(ki_done, 2)
            for t in range(2):
                tr(T1[:, t * P:(t + 1) * P], ki_tok[:, t, :], ident[:])
                tr(T0[:, t * P:(t + 1) * P], cki_tok[:, t, :], ident[:])
            tr(T0[:, PAST:SK], ki_tok[0:TS, 2, :], ident[0:TS, 0:TS]).then_inc(kiT_done, 1)
            pe.wait_ge(kiT_ready, 2)
            with pe.Fori(1, W_QI.loops) as i:
                for u in range(4):
                    unit(W_QI, i, u, KU * u, u == 0, u == 3, SET[1], h_hi, h_lo,
                         free=(act_evac, lambda b: at(ACT_EV, W_QI, i, b - 1)))
                    if u == 0:
                        pe.wait_ge(act_evac, at(ACT_EV, W_QI, i, 0))
                    score_index_head(i - 1, u)

            def conv_units(i, tail=None):
                for u in range(8):
                    g = u // 4
                    free = None
                    if not isinstance(i, int):
                        free = ((act_evac, lambda b: at(ACT_EV, W_CONV, i, b - 1)),
                                (dve_evac, lambda b: at(DVE_EV, W_CONV, i, b - 1)))[g]
                    if isinstance(i, int) and u == 4:
                        pe.wait_ge(act_evac, at(ACT_EV, W_CONV, 0, 0))
                    unit(W_CONV, i, u, KU * (u % 4), u % 4 == 0, u % 4 == 3, SET[g], h_hi, h_lo, free=free)
                    if tail is not None:
                        tail(u)

            def last_index_heads(u):
                if u < 4:
                    if u == 0:
                        pe.wait_ge(act_evac, at(ACT_EV, W_CONV, 0, 0))
                    score_index_head(W_QI.loops - 1, u)

            conv_units(0, last_index_heads)
            with pe.Fori(1, W_CONV.loops) as i:
                conv_units(i)
            pe.wait_ge(act_evac, at(ACT_EV, W_HEAD, 0, 0))
            pe.wait_ge(dve_evac, at(DVE_EV, W_HEAD, 0, 0))

            def attend(p, step):
                hh = step in ("scores 1", "probs 1", "out 1")
                b = scr[int(hh)]
                if step == "cached keys":
                    pe.wait_ge(ck_full, 16 * p + 16)
                    pe.wait_ge(o_lo_done, 2 * p + 1)
                    for h in range(2):
                        for t in range(2):
                            done = tr(T0[:, (2 * h + t) * P:(2 * h + t + 1) * P], ck_tok[:, t, h * P:(h + 1) * P],
                                      ident[:])
                    done.then_inc(ck_T_done, 1)
                elif step in ("scores 0", "scores 1"):
                    h = int(hh)
                    pe.wait_ge(t_evac, 9 * p + 1)
                    pe.wait_ge(scored, 2 * p + h + 1)
                    mm(S0[:, 0:P], qT[:, h, 0:P], kT[:, h, 0:P], start=True, stop=True)
                    mm(S0[:, P:P + TP], qT[:, h, P:TP], kT[:, h, 0:TP], start=True, stop=True)
                    mm(S1[0:TS, 0:PAST], qT[:, h, TP:T], ck_T[:, h, :], start=True, stop=True)
                    mm(S1[0:TS, PAST:SK], qT[:, h, TP:T], kT[:, h, TP:T], start=True, stop=True)\
                        .then_inc(scores_done, 1)
                elif step in ("values", "keys"):
                    src, sig, k = (vT, v_T_done, 1) if step == "values" else (kT, k_T_done, 3)
                    pe.wait_ge(t_evac, 9 * p + k)
                    for t in range(2):
                        for h in range(2):
                            done = tr(T1[:, t * NU + h * P:t * NU + (h + 1) * P], src[:, h, t * P:(t + 1) * P],
                                      ident[:])
                    done.then_inc(sig, 1)
                    for h in range(2):
                        done = tr(T0[0:TS, h * P:(h + 1) * P], src[:, h, TP:T], ident[:])
                    done.then_inc(sig, 1)
                elif step in ("probs 0", "probs 1"):
                    pe.wait_ge(p_ready, 2 * p + hh + 1)
                    pe.wait_ge(t_evac, 9 * p + (7 if hh else 5))
                    pe.wait_ge(o_lo_done, 2 * p + hh + 1)
                    tr(T1[:, 0:P], b[:, 0:P], ident[:])
                    tr(T1[:, P:2 * P], b[:, P:2 * P], ident[:])
                    tr(T1[:, 2 * P:3 * P], b[:, 2 * P:3 * P], ident[:]).then_inc(pT_done, 1)
                    c0 = P + TP
                    tr(T0[:, 0:TS], b[0:TS, c0:c0 + P], ident[0:TS, 0:TS])
                    tr(T0[:, TS:2 * TS], b[0:TS, c0 + P:c0 + 2 * P], ident[0:TS, 0:TS])
                    tr(T0[0:TS, 2 * TS:3 * TS], b[0:TS, c0 + 2 * P:c0 + SK], ident[0:TS, 0:TS]).then_inc(pT_done, 1)
                else:
                    h = int(hh)
                    pe.wait_ge(t_evac, 9 * p + (9 if h else 7))
                    pe.wait_ge(cv_full, 16 * p + 16)
                    pe.wait_ge(o_lo_done, 2 * p + h + 1)
                    hc = slice(h * P, (h + 1) * P)
                    out = T0[:, 3 * TS:3 * TS + T]
                    mm(out[:, 0:TP], v_tok[:, 0, hc], pT[:, 0:TP], start=True, stop=False)
                    mm(out[:, P:TP], v_tok[:, 1, hc], pT[:, TP:TP + P], start=False, stop=True)
                    c0 = TP + P
                    mm(out[:, TP:T], cv_tok[:, 0, hc], pT[:, c0:c0 + TS], start=True, stop=False)
                    mm(out[:, TP:T], cv_tok[:, 1, hc], pT[:, c0 + TS:c0 + 2 * TS], start=False, stop=False)
                    mm(out[:, TP:T], v_tok[0:TS, 2, hc], pT[0:TS, c0 + 2 * TS:c0 + 3 * TS], start=False, stop=True)\
                        .then_inc(pv_done, 1)

            pe.sem_inc(pv_done, 1)

            def head_units(i, extra):
                for u in range(12):
                    g = u // 4
                    free = None
                    if g == 0 and not isinstance(i, int):
                        free = (act_evac, lambda b: at(ACT_EV, W_HEAD, i, b - 1))
                    if g == 2:
                        free = (act_evac, lambda b: at(ACT_EV, W_HEAD, i, b + 1))
                    unit(W_HEAD, i, u, KU * (u % 4), u % 4 == 0, u % 4 == 3, SET[g % 2], h_hi, h_lo, free=free)
                    extra(u)

            def conv_tail(u):
                if u < 2:
                    c0 = (TP, UW - PAD)[u]
                    for c in range(KC):
                        bank = ((T0, T1), (S0, S1))[u][c // 4]
                        done = tr(bank[0:PAD, (c % 4) * P:(c % 4 + 1) * P], u_all[:, c, c0:c0 + PAD], ident[:])
                        if c % 4 == 3:
                            done.then_inc(conv_tail_T, 1)

            head_units(0, conv_tail)
            pe.wait_ge(conv_rows_ready, 4)
            with pe.Fori(1, PAIRS) as i:
                def extra(u):
                    if u < len(HEAD_STEPS):
                        if u == 1:
                            pe.wait_ge(act_evac, at(ACT_EV, W_HEAD, i, 0))
                        attend(i - 1, HEAD_STEPS[u])
                head_units(i, extra)
            pe.wait_ge(act_evac, at(ACT_EV, W_MERGE, 0, 0))

            def merge_units(i, extra=None):
                for u in range(14):
                    g = u // 4
                    free = None
                    if g < 2 and not isinstance(i, int):
                        free = (dve_evac, lambda b: at(DVE_EV, W_MERGE, i, 2 * g + b - 3))
                    if g == 1 and isinstance(i, int) and u == 4:
                        pe.wait_ge(centred, 1)
                    if g >= 2:
                        free = (act_evac, lambda b: at(ACT_EV, W_MERGE, i, 2 * (g - 2) + b + 1))
                    hi, lo = ((h_hi, h_lo), (h_hi, h_lo), (o_hi, o_lo), (s_hi, s_lo))[g]
                    part = (o_lo_done, H + 1) if u == 8 else (s_ready, u - 11) if u >= 12 else None
                    last = u in (3, 7, 11, 13)
                    unit(W_MERGE, i, u, KU * (u % 4), u % 4 == 0, last, SET[g % 2], hi, lo, free=free, part=part)
                    if extra is not None:
                        extra(u)

            def last_pair_and_norm(u):
                for step in HEAD_STEPS[u:u + 1] if u < 7 else HEAD_STEPS[7:] if u == 7 else ():
                    attend(PAIRS - 1, step)
                if u == 0:
                    pe.wait_ge(conv_done, KC)
                    for c in range(KC):
                        done = mm(M[2][:, 0:T], ones[:], c_all[:, c, :], start=c == 0, stop=c == KC - 1)
                    done.then_inc(mean_done, 1)
                if u == 5:
                    pe.wait_ge(squared, KC)
                    pe.wait_ge(scored, H + 1)
                    for c in range(KC):
                        done = mm(S0[:, 0:T], ones[:], c_sq[:, c, :], start=c == 0, stop=c == KC - 1)
                    done.then_inc(var_done, 1)

            merge_units(0, last_pair_and_norm)
            with pe.Fori(1, W_MERGE.loops) as i:
                merge_units(i)

            with pe.Fori(0, W_OUT.loops) as i:
                for u in range(8):
                    g = u // 4
                    unit(W_OUT, i, u, KU * (u % 4), u % 4 == 0, u % 4 == 3, SET[g], h_hi, h_lo,
                         free=(dve_evac, lambda b: at(DVE_EV, W_OUT, i, 2 * g + b - 3)),
                         part=(h_ready, 4 + u + 1) if g == 0 else None)

            def sum_squares(n):
                pe.wait_ge(ssq_added, KD * n + 2)
                mm(T0[:, 0:T], ones[:], ssq[:], start=True, stop=True).then_inc(ssq_sum, 1)

            sum_squares(1)
            for up, down, nk in ((W_UPA, W_DNA, KFA), (W_UPB, W_DNB, KFB)):
                pe.wait_ge(dve_evac, at(DVE_EV, up, 0, 0))
                with pe.Fori(0, up.loops) as i:
                    for u in range(8):
                        g = u // 4
                        free = ((act_evac, lambda b: at(ACT_EV, up, i, b - 1)),
                                (dve_evac, lambda b: at(DVE_EV, up, i, b - 1)))[g]
                        unit(up, i, u, KU * (u % 4), u % 4 == 0, u % 4 == 3, SET[g], h_hi, h_lo, free=free,
                             part=(h_ready, 8 + u + 1) if g == 0 else None)
                pe.wait_ge(act_lo_ready, nk if up is W_UPA else KF)
                pe.wait_ge(act_evac, at(ACT_EV, down, 0, 0))
                with pe.Fori(0, down.loops) as i:
                    for u in range(nk // KU):
                        unit(down, i, u, KU * u, u == 0, u == nk // KU - 1, SET[0], act_hi, act_lo,
                             free=(dve_evac, lambda b: at(DVE_EV, down, i, b - 1)))
            sum_squares(2)
            for j in range(KD):
                pe.wait_ge(y_ready, j + 1)
                if j >= 2:
                    pe.wait_ge(y_evac, j - 1)
                bank = (T1, S0)[j % 2]
                for t, c, n in TOK:
                    done = tr(bank[0:n, t * P:(t + 1) * P], y_c[:, j % 2, c:c + n], ident[:])
                done.then_inc(y_T, 1)

        @block.scalar
        def _(act):
            act_fn = nc.scalar.activation
            step = Steps()
            act.sem_inc(relu_done, 1)

            def high_half(ph, i, u):
                if u >= ph.n:
                    i, u = i + 1, u - ph.n
                n = KU * NKI if ph is W_KI else KU * NU
                s = u % 4
                act.wait_ge(raw_full[s], 16 * ph.fills(i, u))
                if ph.freed(i, u) is not None:
                    act.wait_ge(units_used, ph.freed(i, u))
                act_fn(w_hi[:, s, 0:n], w_raw[:, s, 0:n], ACT.Copy).then_inc(hi_ready, 1)

            def group_tile(ph, i, u, g, b):
                if b == 0:
                    act.wait_ge(first_done, at(GROUPS, ph, i, g + 1))
                else:
                    act.wait_ge(units_used, ph.count(i, u))

            act.wait_ge(x_in, 32)
            act.wait_ge(dve_step, 1)
            for t, n in ((0, P), (1, P), (2, TS)):
                act_fn(junk[0:n, :], x_tok[0:n, t, :], ACT.Square, accum_out=stat[0:n, t:t + 1]).then_inc(act_step, 1)
                act.wait_ge(act_step, step.up())
            act.wait_ge(consts, 4)
            act_fn(stat[:, 3:5], stat[:, 0:2], ACT.Sqrt, bias=eps[:], scale=1.0 / D).then_inc(x_std, 1)
            act_fn(stat[0:TS, 5:6], stat[0:TS, 2:3], ACT.Sqrt, bias=eps[0:TS], scale=1.0 / D).then_inc(x_std, 1)
            act.wait_ge(rows_T, 1)
            act_fn(vecs[:], S0[:, 0:NV], ACT.Copy).then_inc(vecs_ready, 1)
            high_half(W_KI, 0, 0)
            high_half(W_KI, 0, 1)

            def split_high(n, src):
                for q in range(4):
                    if src is None:
                        act.wait_ge(hf_ready, 4 * (n // 2) + q + 1)
                    act_fn(h_hi[:, 4 * q:4 * q + 4, :], hf[q % 2][:] if src is None else src[:, 4 * q:4 * q + 4, :],
                           ACT.Copy).then_inc(h_hi_ready, 1)

            split_high(0, None)

            for u in range(4):
                if u < 2:
                    high_half(W_KI, 0, u + 2)
                else:
                    high_half(W_QI, 0, u - 2)
            act.wait_ge(units_used, W_KI.count(0, 3))
            act_fn(kiw[0:NKI, :], M[0][0:NKI, 0:T], ACT.Copy).then_inc(act_evac, 1)

            def evac(ph, i, u, g, dst, fn, wait=None):
                for b in range(2):
                    group_tile(ph, i, u, g, b)
                    if wait is not None and b == 0:
                        act.wait_ge(*wait)
                    act_fn(dst[:, b, :], SET[BANK[ph][g]][b][:, 0:T], fn).then_inc(act_evac, 1)

            BANK = {W_QI: [1], W_CONV: [0, 1], W_HEAD: [0, 1, 0], W_MERGE: [0, 1, 0, 1], W_UPA: [0, 1], W_UPB: [0, 1]}

            def relu_head(p, hh):
                act.wait_ge(idx_scored, 4 * p + (hh + 1))
                act.wait_ge(score_added, 4 * p + (hh + 1))
                r = relu_sc[hh % 2]
                act_fn(r[0:TS, P + TP:SW], S1[0:TS, 0:SK], ACT.Relu, scale=IDX_SCALE).then_inc(act_step, 1)
                act.wait_ge(act_step, step.up())
                act_fn(r[:, 0:P + TP], S0[:, 0:P + TP], ACT.Relu, scale=IDX_SCALE).then_inc(relu_done, 1)

            for u in range(4):
                high_half(W_QI, 0, u + 2)
                if u == 0:
                    act.wait_ge(ki_var, 3)
                    act_fn(istd[:], mv[:, :, 1], ACT.Sqrt, bias=eps[:]).then_inc(ki_std, 1)
            evac(W_QI, 0, 3, 0, qiT, ACT.Copy)
            act.wait_ge(kiT_done, 1)
            act_fn(kiT[:, 0:TP], T1[:, 0:TP], ACT.Copy).then_inc(kiT_ready, 1)
            act_fn(kiT[:, TP:TP + SK], T0[:, 0:SK], ACT.Copy).then_inc(kiT_ready, 1)
            with act.Fori(1, W_QI.loops) as i:
                step.enter(i, 4, 1)
                for u in range(4):
                    high_half(W_QI, i, u + 2)
                    relu_head(i - 1, u)
                evac(W_QI, i, 3, 0, qiT, ACT.Copy)
                step.leave(W_QI.loops - 1)

            for i0 in (0, 1):
                loop = ExitStack()
                i = 0 if i0 == 0 else loop.enter_context(act.Fori(1, W_CONV.loops))
                for u in range(8):
                    high_half(W_CONV, i, u + 2)
                    if i0 == 0 and u < 4:
                        relu_head(W_QI.loops - 1, u)
                    if u == 3:
                        evac(W_CONV, i, 3, 0, sig_b, ACT.Sigmoid,
                             None if i0 == 0 else (dve_evac, at(DVE_EV, W_CONV, i, 0)))
                loop.close()

            def attend(p, u):
                if u == 0:
                    act.wait_ge(ck_T_done, p + 1)
                    act_fn(ck_T[:].rearrange("p h t -> p (h t)"), T0[:, 0:2 * PAST], ACT.Copy).then_inc(t_evac, 1)
                if u in (2, 3):
                    h = u - 2
                    act.wait_ge(rec_ready, 2 * p + h + 1)
                    act_fn(scr[h][:, 0:P], scr[h][:, 0:P], ACT.Copy, scale=srec[:, h, 0:1]).then_inc(act_step, 1)
                    step.up()
                    act_fn(scr[h][:, P:P + TP], scr[h][:, P:P + TP], ACT.Copy, scale=srec[:, h, 1:2])\
                        .then_inc(act_step, 1)
                    act.wait_ge(act_step, step.up())
                    act_fn(scr[h][0:TS, P + TP:SW], scr[h][0:TS, P + TP:SW], ACT.Copy, scale=srec[0:TS, h, 2:3])\
                        .then_inc(p_ready, 1)
                if u in (1, 2):
                    h = u - 1
                    act.wait_ge(scored, 2 * p + h + 2)
                    for t, c, n, w in ((0, 0, P, P), (1, P, P, TP), (2, P + TP, TS, SK)):
                        act_fn(scr[h][0:n, c:c + w], scr[h][0:n, c:c + w], ACT.Exp, bias=snmax[0:n, h, t:t + 1],
                               accum_out=ssum[0:n, h, t:t + 1]).then_inc(exp_done, 1)
                if u in (3, 4):
                    sig, tok = ((v_T_done, v_tok), (k_T_done, k_tok))[u - 3]
                    act.wait_ge(kv_stored, p + 1)
                    act.wait_ge(sig, 2 * p + 1)
                    act_fn(tok[:, 0:2, :].rearrange("p t c -> p (t c)"), T1[:, 0:2 * NU], ACT.Copy)\
                        .then_inc(t_evac, 1)
                    act.wait_ge(sig, 2 * p + 2)
                    act_fn(tok[0:TS, 2, :], T0[0:TS, 0:NU], ACT.Copy).then_inc(t_evac, 1)
                if u in (5, 7):
                    h = (u - 5) // 2
                    act.wait_ge(pT_done, 4 * p + 2 * h + 1)
                    act.wait_ge(pv_done, 2 * p + h + 1)
                    act_fn(pT[:, 0:TP + P], T1[:, 0:TP + P], ACT.Copy).then_inc(t_evac, 1)
                    act.wait_ge(pT_done, 4 * p + 2 * h + 2)
                    act_fn(pT[:, TP + P:TP + P + 2 * TS], T0[:, 0:2 * TS], ACT.Copy).then_inc(act_step, 1)
                    step.up()
                    act_fn(pT[0:TS, TP + P + 2 * TS:PW], T0[0:TS, 2 * TS:3 * TS], ACT.Copy).then_inc(t_evac, 1)
                if u in (6, 8):
                    h = (u - 6) // 2
                    if h == 0:
                        act.wait_ge(conv_tail_out, 32)
                    act.wait_ge(pv_done, 2 * p + h + 2)
                    act_fn(o_hi[:, ds(2 * p + h, 1), :], T0[:, 3 * TS:3 * TS + T], ACT.Copy).then_inc(o_hi_done, 1)

            ATT_STEPS = 6

            for i0 in (0, 1):
                loop = ExitStack()
                i = 0 if i0 == 0 else loop.enter_context(act.Fori(1, PAIRS))
                if i0:
                    step.enter(i, ATT_STEPS, 1)
                for u in range(12):
                    high_half(W_HEAD, i, u + 2)
                    if i0:
                        attend(i - 1, u)
                    if i0 == 0 and u < 2:
                        for half, bank in enumerate(((T0, T1), (S0, S1))[u]):
                            act.wait_ge(conv_tail_T, 2 * u + half + 1)
                            act_fn(conv_rows_out[:, u, half * 512:(half + 1) * 512], bank[0:PAD, :], ACT.Copy)\
                                .then_inc(conv_rows_ready, 1)
                    if u % 4 == 3:
                        g = u // 4
                        wait = None
                        if i0:
                            wait = ((scores_done, 2 * i), (k_T_done, 2 * i), (v_T_done, 2 * i))[g]
                        evac(W_HEAD, i, u, g, (qT, kT, vT)[g], ACT.Copy, wait)
                if i0:
                    step.leave(PAIRS - 1)
                loop.close()

            for i0 in (0, 1):
                loop = ExitStack()
                i = 0 if i0 == 0 else loop.enter_context(act.Fori(1, W_MERGE.loops))
                for u in range(14):
                    high_half(W_MERGE, i, u + 2)
                    for n in () if i0 or u > 7 else (7, 8) if u == 7 else (u,):
                        attend(PAIRS - 1, n)
                    if i0 == 0 and u == 3:
                        for c in range(KC):
                            act.wait_ge(centred, c + 1)
                            act_fn(c_sq[:, c, :], c_all[:, c, :], ACT.Square).then_inc(squared, 1)
                    if i0 == 0 and u == 8:
                        act.wait_ge(var_done, 1)
                        act_fn(rstd0[:], S0[:, 0:T], ACT.Sqrt, bias=eps[:], scale=1.0 / DC).then_inc(ln_std, 1)
                        for c in range(KC):
                            act.wait_ge(s_scaled, c + 1)
                            act_fn(c_all[:, c, :], c_all[:, c, :], ACT.Silu, bias=LN_B[:, c:c + 1],
                                   scale=LN_G[:, c:c + 1]).then_inc(s_f_ready, 1)
                            if c % 4 == 3:
                                act.wait_ge(s_f_ready, c + 1)
                                act.wait_ge(kv_stored, PAIRS + 1)
                                act_fn(s_hi[:, c - 3:c + 1, :], c_all[:, c - 3:c + 1, :], ACT.Copy)\
                                    .then_inc(s_hi_ready, 1)
                    if u in (3, 7):
                        g = u // 4
                        wait = None if i0 == 0 else (dve_evac, at(DVE_EV, W_MERGE, i, 0))
                        evac(W_MERGE, i, u, g, (sig_a, sig_g)[g], ACT.Sigmoid, wait)
                loop.close()
            act.wait_ge(dve_evac, at(DVE_EV, W_OUT, 0, 0))
            act.wait_ge(m_done, 2 * W_MERGE.loops)
            split_high(1, m_all)

            with act.Fori(0, W_OUT.loops) as i:
                for u in range(8):
                    high_half(W_OUT, i, u + 2)
                    if u % 4 == 3:
                        for b in range(2):
                            k = 2 * (u // 4) + b
                            act.wait_ge(dve_evac, at(DVE_EV, W_OUT, i, k + 1))
                            act.wait_ge(ssq_added, i * 4 + (k + 1))
                            act_fn(sq[:, b, :], xT[:, ds(i * 4 + k, 1), :], ACT.Square).then_inc(x_squared, 1)

            def norm_root(n):
                act.wait_ge(ssq_sum, n)
                act_fn(rstd[:], T0[:, 0:T], ACT.Sqrt, bias=eps[:], scale=1.0 / D).then_inc(norm_std, 1)

            norm_root(1)
            split_high(2, None)
            for up, down, nk, k0 in ((W_UPA, W_DNA, KFA, 0), (W_UPB, W_DNB, KFB, KFA)):
                with act.Fori(0, up.loops) as i:
                    for u in range(8):
                        high_half(up, i, u + 2)
                        if u == 3:
                            evac(up, i, u, 0, silu_g, ACT.Silu, (dve_evac, at(DVE_EV, up, i, 0)))
                        if u == 7:
                            for b in range(2):
                                act.wait_ge(dve_evac, at(DVE_EV, up, i, b + 1))
                                act_fn(act_hi[:, ds(i * 2 + b, 1), :], act_f[:, b, :], ACT.Copy)\
                                    .then_inc(act_hi_ready, 1)
                n = nk // KU
                if down is W_DNA:
                    with act.Fori(0, down.loops) as i:
                        for u in range(n):
                            high_half(down, i, u + 2)
                else:
                    for i0 in (0, 1):
                        loop = ExitStack()
                        i = down.loops - 1 if i0 else loop.enter_context(act.Fori(0, down.loops - 1))
                        for u in range(n):
                            if not i0 or u + 2 < n:
                                high_half(down, i, u + 2)
                        for b in range(2):
                            act.wait_ge(dve_evac, at(DVE_EV, down, i, b + 1))
                            act.wait_ge(ssq_added, i * 2 + (KD + b + 1))
                            act_fn(sq[:, b, :], xT[:, ds(i * 2 + b, 1), :], ACT.Square).then_inc(x_squared, 1)
                        loop.close()
            norm_root(2)
            for j in range(KD):
                act.wait_ge(y_T, j + 1)
                bank = (T1, S0)[j % 2]
                act_fn(y_tok[:, 0:2, j * P:(j + 1) * P], bank[:, 0:2 * P].rearrange("p (t c) -> p t c", c=P),
                       ACT.Copy).then_inc(act_step, 1)
                step.up()
                act_fn(y_tok[0:TS, 2, j * P:(j + 1) * P], bank[0:TS, 2 * P:3 * P], ACT.Copy).then_inc(y_evac, 1)

        @block.vector
        def _(dve):
            v = nc.vector
            step = Steps()

            def low_half(ph, i, u):
                if u >= ph.n:
                    i, u = i + 1, u - ph.n
                n = KU * NKI if ph is W_KI else KU * NU
                s = u % 4
                dve.wait_ge(hi_ready, ph.count(i, u))
                v.tensor_tensor(w_lo[:, s, 0:n], w_raw[:, s, 0:n], w_hi[:, s, 0:n].bitcast(f32), ALU.subtract)\
                    .then_inc(lo_ready, 1)

            def group_tile(ph, i, u, g, b):
                if b == 0:
                    dve.wait_ge(first_done, at(GROUPS, ph, i, g + 1))
                else:
                    dve.wait_ge(units_used, ph.count(i, u))

            dve.sem_inc(scored, 1)
            dve.sem_inc(o_lo_done, 1)
            dve.sem_inc(ssq_added, 2)
            dve.sem_inc(score_added, 2)
            v.memset(stat[:], 1.0).then_inc(dve_step, 1)
            step.up()
            v.memset(mv[:], 1.0).then_inc(dve_step, 1)
            step.up()
            v.memset(bn[:], 0.0).then_inc(dve_step, 1)
            step.up()
            v.memset(score[:], 0.0).then_inc(dve_step, 1)
            step.up()

            for k in range(KD):
                dve.wait_ge(x_T, k + 1)
                v.tensor_copy(xT[:, k, :], M[k % 4][:, 0:T]).then_inc(x_evac, 1)
                if k == 3:
                    dve.wait_ge(conv_T, 1)
                    v.tensor_copy(conv_w[:, :, 0:TAPS], S1[:, 0:KC * TAPS].rearrange("p (c t) -> p c t", t=TAPS))\
                        .then_inc(dve_step, 1)
                    step.up()
                    dve.wait_ge(cache_T, 1)
                    v.tensor_copy(u_all[:, :, PAD + TP:2 * PAD + TP],
                                  T1[:, 0:KC * PAD].rearrange("p (c t) -> p c t", t=PAD)).then_inc(dve_step, 1)
                    step.up()
            dve.wait_ge(x_std, 2)
            dve.wait_ge(consts, 4)
            v.reciprocal(stat[:, 3:6], stat[:, 3:6]).then_inc(dve_step, 1)
            dve.wait_ge(dve_step, step.up())
            for t in range(3):
                done = v.tensor_scalar(diag[:, t, :], ident[:], stat[:, 3 + t:4 + t], None, ALU.mult)
            done.then_inc(diag_ready, 1)
            dve.wait_ge(vecs_ready, 1)
            v.tensor_copy(conv_w[:, :, TAPS:TAPS + 1], CONV_B.unsqueeze(2)).then_inc(dve_step, 1)
            step.up()
            dve.wait_ge(rstd_sum, 1)
            v.tensor_copy(rstd0[:], T0[:, 0:T]).then_inc(dve_step, 1)
            dve.wait_ge(dve_step, step.up())

            def low_of_h(n, q, src):
                dve.wait_ge(h_hi_ready, 4 * n + q + 1)
                v.tensor_tensor(h_lo[:, 4 * q:4 * q + 4, :], src, h_hi[:, 4 * q:4 * q + 4, :].bitcast(f32),
                                ALU.subtract).then_inc(h_ready, 1)

            def normalise(n, g, r):
                for q in range(5):
                    if q < 4:
                        if q >= 2:
                            dve.wait_ge(h_ready, 4 * n + q - 1)
                        for j in range(4):
                            k = 4 * q + j
                            done = v.scalar_tensor_tensor(out=hf[q % 2][:, j, :], in0=xT[:, k, :], scalar=g[:, k:k + 1],
                                                          in1=r, op0=ALU.mult, op1=ALU.mult)
                        done.then_inc(hf_ready, 1)
                    if q >= 1:
                        low_of_h(n, q - 1, hf[(q - 1) % 2][:])

            low_half(W_KI, 0, 0)
            low_half(W_KI, 0, 1)
            normalise(0, G_MIX, rstd0[:])

            for u in range(4):
                if u < 2:
                    low_half(W_KI, 0, u + 2)
                else:
                    low_half(W_QI, 0, u - 2)

            ROWS = ((0, P), (1, P), (2, TS))
            for u in range(4):
                low_half(W_QI, 0, u + 2)
                if u == 0:
                    dve.wait_ge(kiw_T, 1)
                    dve.wait_ge(idx_in, 64)
                    for t, n in ROWS:
                        v.bn_stats(bn[0:n, t, :], T0[0:n, t * NKI:t * NKI + DI]).then_inc(dve_step, 1)
                        dve.wait_ge(dve_step, step.up())
                    for t, n in ROWS:
                        v.bn_aggr(mv[0:n, t, :], bn[0:n, t, :]).then_inc(ki_var, 1)
                    for t, n in ROWS:
                        v.tensor_copy(w_tok[0:n, t, :], T0[0:n, t * NKI + DI:(t + 1) * NKI]).then_inc(dve_step, 1)
                        step.up()
                    dve.wait_ge(ki_std, 1)
                    v.reciprocal(istd[:], istd[:]).then_inc(dve_step, 1)
                    dve.wait_ge(dve_step, step.up())
                if u == 1:
                    for t, n in ROWS:
                        k = ki_tok[0:n, t, 0:DI]
                        v.tensor_scalar(k, T0[0:n, t * NKI:t * NKI + DI], mv[0:n, t, 0:1], istd[0:n, t:t + 1],
                                        ALU.subtract, ALU.mult).then_inc(dve_step, 1)
                        dve.wait_ge(dve_step, step.up())
                        v.tensor_tensor(k, k, idx_g[0:n, :], ALU.mult).then_inc(dve_step, 1)
                        dve.wait_ge(dve_step, step.up())
                        v.tensor_tensor(k, k, idx_b[0:n, :], ALU.add).then_inc(dve_step, 1)
                        dve.wait_ge(dve_step, step.up())
                    v.tensor_copy(ki_tok[:, 0:2, DI:2 * DI], ki_tok[:, 0:2, 0:DI]).then_inc(ki_done, 1)
                    v.tensor_copy(ki_tok[0:TS, 2, DI:2 * DI], ki_tok[0:TS, 2, 0:DI]).then_inc(ki_done, 1)

            SPAN = ((0, 0, P, P), (1, P, P, TP), (2, P + TP, TS, SK))

            def add_head(p, hh):
                if hh == 0:
                    dve.wait_ge(score_added, 4 * p + 2)
                    v.tensor_copy(w_grp[:, 0:2, :], w_tok[:, 0:2, ds(4 * p, 4)]).then_inc(dve_step, 1)
                    step.up()
                    v.tensor_copy(w_grp[0:TS, 2, :], w_tok[0:TS, 2, ds(4 * p, 4)]).then_inc(dve_step, 1)
                    dve.wait_ge(dve_step, step.up())
                dve.wait_ge(relu_done, 4 * p + (hh + 2))
                dve.wait_ge(score_added, 4 * p + (hh + 2))
                r = relu_sc[hh % 2]
                for t, c, n, w in SPAN:
                    done = v.scalar_tensor_tensor(out=score[0:n, c:c + w], in0=r[0:n, c:c + w],
                                                  scalar=w_grp[0:n, t, hh:hh + 1], in1=score[0:n, c:c + w],
                                                  op0=ALU.mult, op1=ALU.add)
                done.then_inc(score_added, 1)

            with dve.Fori(1, W_QI.loops) as i:
                step.enter(i, 2, 1)
                for u in range(4):
                    low_half(W_QI, i, u + 2)
                    add_head(i - 1, u)
                step.leave(W_QI.loops - 1)

            for i0 in (0, 1):
                loop = ExitStack()
                i = 0 if i0 == 0 else loop.enter_context(dve.Fori(1, W_CONV.loops))
                if i0:
                    step.enter(i, 2, 1)
                for u in range(8):
                    low_half(W_CONV, i, u + 2)
                    if i0 == 0 and u < 4:
                        add_head(W_QI.loops - 1, u)
                for b in range(2):
                    dve.wait_ge(act_evac, at(ACT_EV, W_CONV, i, b + 1))
                    group_tile(W_CONV, i, 7, 1, b)
                    v.tensor_tensor(u_all[:, ds(2 * i + b, 1), PAD:PAD + TP], SET[1][b][:, 0:TP],
                                    sig_b[:, b, 0:TP], ALU.mult).then_inc(dve_step, 1)
                    step.up()
                    v.tensor_tensor(u_all[:, ds(2 * i + b, 1), 2 * PAD + TP:UW], SET[1][b][:, TP:T],
                                    sig_b[:, b, TP:T], ALU.mult).then_inc(dve_evac, 1)
                if i0:
                    step.leave(W_CONV.loops - 1)
                loop.close()

            TAPS_AT = [3] * 9 + [2, 2, 0]
            assert sum(TAPS_AT) == TAPS

            def convolve(i, u):
                if u == 0:
                    v.tensor_copy(u_cur[:], u_all[:, ds(i, 1), :]).then_inc(dve_step, 1)
                    step.up()
                    v.tensor_copy(w_cur[:], conv_w[:, ds(i, 1), :]).then_inc(dve_step, 1)
                    dve.wait_ge(dve_step, step.up())
                first = sum(TAPS_AT[:u])
                for t in range(first, first + TAPS_AT[u]):
                    if t == 0:
                        v.tensor_scalar(acc[:], u_cur[:, 0:CW], w_cur[:, 0:1], w_cur[:, TAPS:TAPS + 1],
                                        ALU.mult, ALU.add).then_inc(dve_step, 1)
                    else:
                        v.scalar_tensor_tensor(out=acc[:], in0=u_cur[:, t:t + CW], scalar=w_cur[:, t:t + 1],
                                               in1=acc[:], op0=ALU.mult, op1=ALU.add).then_inc(dve_step, 1)
                    dve.wait_ge(dve_step, step.up())
                if u == 11:
                    v.tensor_copy(c_all[:, ds(i, 1), 0:TP], acc[:, 0:TP]).then_inc(dve_step, 1)
                    step.up()
                    v.tensor_copy(c_all[:, ds(i, 1), TP:T], acc[:, TP + PAD:CW]).then_inc(conv_done, 1)
                    dve.wait_ge(conv_done, i + 1)

            def top_round(r):
                todo = [s for s in SPAN if r < (TOP_S if s[0] == 2 else TOP_P) // 8]
                for t, c, n, w in todo:
                    v.max(top8[0:n, t, :], score[0:n, c:c + w]).then_inc(dve_step, 1)
                    step.up()
                for j, (t, c, n, w) in enumerate(todo):
                    dve.wait_ge(dve_step, step.now() - (len(todo) - 1))
                    v.match_replace(score[0:n, c:c + w], top8[0:n, t, :], score[0:n, c:c + w], REMOVED)\
                        .then_inc(dve_step, 1)
                    step.up()
                dve.wait_ge(dve_step, step.now())

            CONV_STEPS = 2 + TAPS + 1

            def attend(p, u):
                if u in (2, 3):
                    h = u - 2
                    dve.wait_ge(exp_done, 6 * p + 3 * h + 3)
                    v.reciprocal(srec[:, h, :], ssum[:, h, :]).then_inc(rec_ready, 1)
                if u in (1, 2):
                    h = u - 1
                    dve.wait_ge(scores_done, 2 * p + h + 1)
                    v.memset(ssum[:, h, :], 1.0).then_inc(dve_step, 1)
                    step.up()
                    for (t, c, n, w), bank in zip(SPAN, (S0[:, 0:P], S0[:, P:P + TP], S1[0:TS, 0:SK])):
                        v.tensor_tensor_reduce(out=scr[h][0:n, c:c + w], in0=bank, in1=bias[0:n, c:c + w], scale=SCALE,
                                               scalar=4 * BIG, op0=ALU.add, op1=ALU.max,
                                               accum_out=smax[0:n, h, t:t + 1]).then_inc(dve_step, 1)
                        done = step.up()
                    dve.wait_ge(dve_step, done)
                    v.tensor_scalar(snmax[:, h, :], smax[:, h, :], -1.0, None, ALU.mult).then_inc(scored, 1)
                if u in (6, 8):
                    h = (u - 6) // 2
                    dve.wait_ge(o_hi_done, 2 * p + h + 1)
                    v.tensor_tensor(o_lo[:, ds(2 * p + h, 1), :], T0[:, 3 * TS:3 * TS + T],
                                    o_hi[:, ds(2 * p + h, 1), :].bitcast(f32), ALU.subtract).then_inc(o_lo_done, 1)

            dve.wait_ge(score_added, HI + 2)
            dve.wait_ge(pads, 1)
            v.memset(score[0:CHUNK, CHUNK:P], OUTSIDE).then_inc(dve_step, 1)
            step.up()
            v.memset(score[0:CHUNK, P + TP - CHUNK:P + TP], OUTSIDE).then_inc(dve_step, 1)
            dve.wait_ge(dve_step, step.up())
            for u in range(12):
                low_half(W_HEAD, 0, u + 2)
                convolve(0, u)
                if u < TOP_S // 8:
                    top_round(u)
                if u == 11:
                    for t, c, n, w in SPAN:
                        v.tensor_scalar(bias[0:n, c:c + w], score[0:n, c:c + w], IS_REMOVED, BIG, ALU.is_gt, ALU.mult)\
                            .then_inc(dve_step, 1)
                        done = step.up()
                    v.memset(smax[:], 0.0).then_inc(dve_step, 1)
                    step.up()
                    dve.wait_ge(dve_step, step.now())
            with dve.Fori(1, PAIRS) as i:
                step.enter(i, CONV_STEPS + 8, 1)
                for u in range(12):
                    low_half(W_HEAD, i, u + 2)
                    attend(i - 1, u)
                    convolve(i, u)
                step.leave(PAIRS - 1)

            for i0 in (0, 1):
                loop = ExitStack()
                i = 0 if i0 == 0 else loop.enter_context(dve.Fori(1, W_MERGE.loops))
                for u in range(14):
                    low_half(W_MERGE, i, u + 2)
                    for n in () if i0 or u > 7 else (7, 8) if u == 7 else (u,):
                        attend(PAIRS - 1, n)
                    if i0 == 0 and u == 1:
                        dve.wait_ge(mean_done, 1)
                        v.tensor_scalar(rstd0[:], M[2][:, 0:T], 1.0 / DC, None, ALU.mult).then_inc(dve_step, 1)
                        dve.wait_ge(dve_step, step.up())
                        for c in range(KC):
                            v.tensor_tensor(c_all[:, c, :], c_all[:, c, :], rstd0[:], ALU.subtract)\
                                .then_inc(centred, 1)
                    if i0 == 0 and u == 8:
                        dve.wait_ge(ln_std, 1)
                        v.reciprocal(rstd0[:], rstd0[:]).then_inc(dve_step, 1)
                        dve.wait_ge(dve_step, step.up())
                        for c in range(KC):
                            v.tensor_tensor(c_all[:, c, :], c_all[:, c, :], rstd0[:], ALU.mult).then_inc(s_scaled, 1)
                            if c % 4 == 3:
                                dve.wait_ge(s_hi_ready, c // 4 + 1)
                                v.tensor_tensor(s_lo[:, c - 3:c + 1, :], c_all[:, c - 3:c + 1, :],
                                                s_hi[:, c - 3:c + 1, :].bitcast(f32), ALU.subtract)\
                                    .then_inc(s_ready, 1)
                    if u == 11:
                        for b in range(2):
                            dve.wait_ge(act_evac, at(ACT_EV, W_MERGE, i, 3 + b))
                            group_tile(W_MERGE, i, 11, 2, b)
                            v.tensor_tensor(m_tmp[:, b, :], M[b][:, 0:T], sig_g[:, b, :], ALU.mult)\
                                .then_inc(dve_evac, 1)
                for b in range(2):
                    group_tile(W_MERGE, i, 13, 3, b)
                    v.tensor_tensor(m_tmp2[:, b, :], M[2 + b][:, 0:T], sig_a[:, b, :], ALU.mult)\
                        .then_inc(dve_evac, 1)
                    dve.wait_ge(dve_evac, at(DVE_EV, W_MERGE, i, 3 + b))
                    v.tensor_tensor(m_all[:, ds(2 * i + b, 1), :], m_tmp[:, b, :], m_tmp2[:, b, :], ALU.add)\
                        .then_inc(m_done, 1)
                loop.close()
            for q in range(4):
                low_of_h(1, q, m_all[:, 4 * q:4 * q + 4, :])

            def add_square(k, b):
                dve.wait_ge(x_squared, k + 1)
                dve.wait_ge(ssq_added, k + 2)
                v.tensor_tensor(ssq[:], ssq[:], sq[:, b, :], ALU.add).then_inc(ssq_added, 1)

            def add_to_x(ph, i, u, g, k, bank, b):
                group_tile(ph, i, u, g, b)
                v.tensor_tensor(xT[:, ds(k, 1), :], bank[:, 0:T], xT[:, ds(k, 1), :], ALU.add).then_inc(dve_evac, 1)

            v.memset(ssq[:], 0.0).then_inc(dve_step, 1)
            dve.wait_ge(dve_step, step.up())
            with dve.Fori(0, W_OUT.loops) as i:
                for u in range(8):
                    low_half(W_OUT, i, u + 2)
                    g = u // 4
                    if u % 4 == 3:
                        for b in range(2):
                            add_to_x(W_OUT, i, u, g, 4 * i + (2 * g + b), SET[g][b], b)
                        for b in range(2):
                            add_square(4 * i + (2 * g + b), b)

            def norm_reciprocal(n):
                dve.wait_ge(norm_std, n)
                v.reciprocal(rstd[:], rstd[:]).then_inc(dve_step, 1)
                dve.wait_ge(dve_step, step.up())

            norm_reciprocal(1)
            normalise(2, G_FFN, rstd[:])

            for up, down, nk, k0 in ((W_UPA, W_DNA, KFA, 0), (W_UPB, W_DNB, KFB, KFA)):
                with dve.Fori(0, up.loops) as i:
                    for u in range(8):
                        low_half(up, i, u + 2)
                    for b in range(2):
                        dve.wait_ge(act_evac, at(ACT_EV, up, i, b + 1))
                        group_tile(up, i, 7, 1, b)
                        v.tensor_tensor(act_f[:, b, :], SET[1][b][:, 0:T], silu_g[:, b, :], ALU.mult)\
                            .then_inc(dve_evac, 1)
                    for b in range(2):
                        dve.wait_ge(act_hi_ready, 2 * i + (k0 + b + 1))
                        v.tensor_tensor(act_lo[:, ds(2 * i + b, 1), :], act_f[:, b, :],
                                        act_hi[:, ds(2 * i + b, 1), :].bitcast(f32), ALU.subtract)\
                            .then_inc(act_lo_ready, 1)
                n = nk // KU
                if down is W_DNA:
                    with dve.Fori(0, down.loops) as i:
                        for u in range(n):
                            low_half(down, i, u + 2)
                        for b in range(2):
                            add_to_x(down, i, n - 1, 0, 2 * i + b, M[b], b)
                else:
                    v.memset(ssq[:], 0.0).then_inc(dve_step, 1)
                    dve.wait_ge(dve_step, step.up())
                    for i0 in (0, 1):
                        loop = ExitStack()
                        i = down.loops - 1 if i0 else loop.enter_context(dve.Fori(0, down.loops - 1))
                        for u in range(n):
                            if not i0 or u + 2 < n:
                                low_half(down, i, u + 2)
                        for b in range(2):
                            add_to_x(down, i, n - 1, 0, 2 * i + b, M[b], b)
                        for b in range(2):
                            add_square(2 * i + (KD + b), b)
                        loop.close()

            norm_reciprocal(2)
            for j in range(KD):
                if j >= 2:
                    dve.wait_ge(y_T, j - 1)
                v.scalar_tensor_tensor(out=y_c[:, j % 2, :], in0=xT[:, j, :], scalar=G_FIN[:, j:j + 1],
                                       in1=rstd[:], op0=ALU.mult, op1=ALU.mult).then_inc(y_ready, 1)


_INS = ["x_prompt", "x_sample", "cache_conv", "cache_k", "cache_v", "cache_kidx", "g_mix", "w_in", "conv_w",
        "conv_b", "conv_ln_g", "conv_ln_b", "w_conv_out", "idx_ln_g", "idx_ln_b", "w_attn_out", "w_out",
        "g_ffn", "w_gate", "w_up", "w_down", "g_final"]


def kernel(**inputs):
    import numpy as np
    import concourse.bacc as bacc
    from concourse.bass_utils import run_bass_kernel_spmd

    nc = bacc.Bacc("TRN2", target_bir_lowering=False, num_devices=1)
    arrays, a = {}, {}
    for name in _INS:
        x = np.ascontiguousarray(inputs[name])
        arrays[f"in_{name}"] = x
        a[name] = nc.dram_tensor(f"in_{name}", x.shape, mybir.dt.from_np(x.dtype), kind="ExternalInput").ap()
    b, tp, d = inputs["x_prompt"].shape
    ts = inputs["x_sample"].shape[1]
    depth, taps, dc = inputs["conv_w"].shape
    heads, hd = inputs["cache_k"].shape[3:]
    di = inputs["cache_kidx"].shape[3]
    shapes = {"y_prompt": (b, tp, d), "y_sample": (b, ts, d),
              "conv_p": (depth, b, taps - 1, dc), "k_p": (depth, b, tp, heads, hd), "v_p": (depth, b, tp, heads, hd),
              "kidx_p": (depth, b, tp, di),
              "conv_s": (depth, b, taps - 1, dc), "k_s": (depth, b, ts, heads, hd), "v_s": (depth, b, ts, heads, hd),
              "kidx_s": (depth, b, ts, di)}
    o = {n: nc.dram_tensor(f"out_{n}", s, mybir.dt.float32, kind="ExternalOutput").ap() for n, s in shapes.items()}
    chunk_causal_conformer_kernel(nc, a, o)
    r = run_bass_kernel_spmd(nc, [arrays], core_ids=[0])
    return tuple(r.results[0][f"out_{n}"] for n in shapes)
```

```python
import concourse.bass as bass
from concourse import mybir
from contextlib import ExitStack


class Stream:
    SLOTS = 4

    def __init__(self, before, loops, n):
        self.n, self.loops = n, loops
        self.start = before.start + before.loops * before.n if before else 0
        self.uses0 = [before.uses0[s] + before.loops * before.per_slot(s) if before else 0
                      for s in range(self.SLOTS)]
        self.before = before

    def per_slot(self, s):
        return len(range(s, self.n, self.SLOTS))

    def count(self, i, u):
        return i * self.n + (self.start + u + 1)

    def fills(self, i, u):
        s = u % self.SLOTS
        return i * self.per_slot(s) + (self.uses0[s] + u // self.SLOTS + 1)

    def freed(self, i, u):
        if u >= self.SLOTS:
            return self.count(i, u - self.SLOTS)
        back = []
        for p in (self, self.before):
            if p is not None and p.per_slot(u):
                last = max(range(u, p.n, self.SLOTS))
                back.append(p.n - last + u)
        if self.before is None:
            return None if isinstance(i, int) and i == 0 else self.count(i, u) - back[0]
        return self.count(i, u) - min(back)


class Steps:

    def __init__(self):
        self.base, self.k, self.per, self.i, self.first = 0, 0, 0, None, 0

    def up(self):
        self.k += 1
        return self.now()

    def now(self):
        n = self.base + self.k
        return n if self.i is None else self.i * self.per + (n - self.first * self.per)

    def enter(self, i, per, first=0):
        self.i, self.per, self.first = i, per, first
        self.base, self.k = self.base + self.k, 0

    def leave(self, trips):
        assert self.k == self.per, (self.k, self.per)
        self.base, self.k, self.i = self.base + trips * self.per, 0, None


def chunk_causal_conformer_kernel(nc, a, o):
    f32, f32r = mybir.dt.float32, mybir.dt.float32r
    ALU, ACT = mybir.AluOpType, mybir.ActivationFunctionType
    ds = bass.ds

    _, TP, D = a["x_prompt"].shape
    TS = a["x_sample"].shape[1]
    T = TP + TS
    PAST, H, HD = a["cache_k"].shape[2:5]
    TAPS, DC = a["conv_w"].shape[1:3]
    PAD = TAPS - 1
    DI = a["cache_kidx"].shape[3]
    HI = 16
    DFF = a["w_gate"].shape[2]
    P = 128
    CHUNK = 64
    EPS = 1e-6
    KD, KC, KF = D // P, DC // P, DFF // P
    KFA = 32
    KFB = KF - KFA
    KU, NU = 4, 256
    SK = PAST + TS
    TOP_P, TOP_S = TP // 4, SK // 4
    assert (TP, TS, PAST, CHUNK, HD, DI) == (256, 64, 256, 64, 128, 64) and TOP_P % 8 == 0 and TOP_S % 8 == 0
    C_A, C_B, C_Q = 0, DC, 2 * DC
    C_K, C_V, C_QI = C_Q + D, C_Q + 2 * D, C_Q + 3 * D
    C_KI = C_QI + HI * DI
    C_GA = C_KI + DI + HI
    C_GB = C_GA + D
    NKI = DI + HI
    PAIRS = H // 2
    SCALE = float(HD) ** -0.5
    IDX_SCALE = float(DI) ** -0.5 * float(HI) ** -0.5
    REMOVED, OUTSIDE, IS_REMOVED, BIG = -3.0e38, -1.0e38, -2.0e38, -1.0e30
    CW = TP + PAD + TS
    UW = PAD + CW

    W_KI = Stream(None, 1, KD // KU)
    W_QI = Stream(W_KI, HI * DI // NU, KD // KU)
    W_CONV = Stream(W_QI, DC // NU, 2 * KD // KU)
    W_HEAD = Stream(W_CONV, PAIRS, 3 * KD // KU)
    W_MERGE = Stream(W_HEAD, D // NU, (3 * KD + KC) // KU)
    W_OUT = Stream(W_MERGE, D // NU // 2, 2 * KD // KU)
    W_UPA = Stream(W_OUT, KFA // 2, 2 * KD // KU)
    W_DNA = Stream(W_UPA, D // NU, KFA // KU)
    W_UPB = Stream(W_DNA, KFB // 2, 2 * KD // KU)
    W_DNB = Stream(W_UPB, D // NU, KFB // KU)

    ACT_EV, DVE_EV, GROUPS = {}, {}, {}
    act_n = dve_n = grp_n = 0
    for ph, per_act, per_dve, per_grp in ((W_KI, 1, 0, 0), (W_QI, 2, 0, 1), (W_CONV, 2, 2, 2), (W_HEAD, 6, 0, 3),
                                          (W_MERGE, 4, 4, 4), (W_OUT, 0, 4, 2), (W_UPA, 0, 4, 2), (W_DNA, 0, 2, 1),
                                          (W_UPB, 0, 4, 2), (W_DNB, 0, 2, 1)):
        ACT_EV[ph], DVE_EV[ph], GROUPS[ph] = (act_n, per_act), (dve_n, per_dve), (grp_n, per_grp)
        act_n += per_act * ph.loops
        dve_n += per_dve * ph.loops
        grp_n += per_grp * ph.loops

    def at(table, ph, i, k):
        base, per = table[ph]
        return i * per + (base + k)

    w_in, w_out = a["w_in"][0], a["w_out"][0]
    w_conv_out, w_attn_out = a["w_conv_out"][0], a["w_attn_out"][0]
    w_gate, w_up, w_down = a["w_gate"][0], a["w_up"][0], a["w_down"][0]

    ctx = ExitStack()
    with ctx:
        place = [(nc.sbuf_base + 31) // 32 * 32]

        def sb(name, shape, dt=f32, offset=None):
            size = 4
            for n in shape[1:]:
                size *= n
            if offset is None:
                offset = place[0]
                place[0] = (offset + size + 31) // 32 * 32
            return nc.alloc_sbuf_tensor_at(name, shape, dt, offset=offset)

        xT = sb("xT", [P, KD, T])
        at_h_hi = place[0]
        h_hi = sb("h_hi", [P, KD, T], f32r)
        at_h_lo = place[0]
        h_lo = sb("h_lo", [P, KD, T], f32r)
        w_raw = sb("w_raw", [P, 4, KU * NU])
        w_hi = sb("w_hi", [P, 4, KU * NU], f32r)
        w_lo = sb("w_lo", [P, 4, KU * NU], f32r)
        ident = sb("ident", [P, P])
        ones = sb("ones", [P, P])
        NV = 3 * KD + 3 * KC
        vecs = sb("vecs", [P, NV])
        G_MIX, G_FFN, G_FIN = vecs[:, 0:KD], vecs[:, KD:2 * KD], vecs[:, 2 * KD:3 * KD]
        CONV_B, LN_G, LN_B = (vecs[:, 3 * KD + j * KC:3 * KD + (j + 1) * KC] for j in range(3))
        conv_w = sb("conv_w_cols", [P, KC, TAPS + 1])
        idx_g = sb("idx_g", [P, DI])
        idx_b = sb("idx_b", [P, DI])
        eps = sb("eps", [P, 1])
        stat = sb("stat", [P, 3])
        stat_v = sb("stat_v", [P, 3])
        stat_r = sb("stat_r", [P, 3])
        stat_t = sb("stat_t", [P, 3])
        bn = sb("bn", [P, 3, 6])
        mv = sb("mv", [P, 3, 2])
        istd = sb("istd", [P, 3])
        top8 = sb("top8", [P, 3, 8])
        smax = sb("smax", [P, 2, 3])
        snmax = sb("snmax", [P, 2, 3])
        ssum = sb("ssum", [P, 2, 3])
        srec = sb("srec", [P, 2, 3])
        at_cur = place[0]
        u_cur = sb("u_cur", [P, UW])
        w_cur = sb("w_cur", [P, TAPS + 1])
        acc = sb("acc", [P, CW])

        A0 = place[0]
        x_tok = sb("x_tok", [P, 3, D], offset=A0)
        at_rows = A0 + 4 * 3 * D
        rows = sb("rows", [NV, P], offset=at_rows)
        conv_w_rows = sb("conv_w_rows", [TAPS, DC], offset=at_rows + 4 * P)
        cache_rows = sb("cache_rows", [PAD, DC], offset=at_rows + 4 * P + 4 * DC)
        assert at_rows + 4 * P + 8 * DC <= A0 + 8 * KD * T
        junk = sb("junk", [P, D], offset=at_h_lo)
        x_scaled = sb("x_scaled", [P, 3, D], offset=A0 + 8 * KD * T)
        o_hi = sb("o_hi", [P, KD, T], f32r, offset=A0)
        o_lo = sb("o_lo", [P, KD, T], f32r, offset=A0 + 4 * KD * T)
        conv_rows_out = sb("conv_rows_out", [PAD, 2, DC], offset=A0)
        A1 = A0 + 8 * KD * T
        u_all = sb("u_all", [P, KC, UW], offset=A1)
        c_all = sb("c_all", [P, KC, T], offset=A1 + 4 * KC * UW)
        A2 = A1 + 4 * KC * (UW + T)
        place[0] = A2
        k_tok = sb("k_tok", [P, 3, NU])
        v_tok = sb("v_tok", [P, 3, NU])
        ck_tok = sb("ck_tok", [P, 2, NU])
        cv_tok = sb("cv_tok", [P, 2, NU])
        ck_T = sb("ck_T", [P, 2, PAST])
        vT = sb("vT", [P, 2, T])
        SW = P + TP + SK
        scr = [sb("scr0", [P, SW]), sb("scr1", [P, SW])]
        bias = sb("bias", [P, SW])
        PW = TP + P + 3 * TS
        pT = sb("pT", [P, PW])
        at_q = place[0]
        qT = sb("qT", [P, 2, T])
        kT = sb("kT", [P, 2, T])
        c_sum = sb("c_sum", [P, T])
        end_attention = place[0]
        place[0] = A2
        kiw = sb("kiw", [P, T])
        ki_tok = sb("ki_tok", [P, 3, 2 * DI])
        kiT = sb("kiT", [P, TP + SK])
        cki_tok = sb("cki_tok", [P, 2, 2 * DI])
        w_tok = sb("w_tok", [P, 3, HI])
        w_grp = sb("w_grp", [P, 3, 4])
        sig_b = sb("sig_b", [P, 2, T], offset=A2 + 8192)
        qiT = sb("qiT", [P, 2, T], offset=A2 + 12288)
        assert place[0] <= A2 + 8192
        score = scr[0]
        relu_sc = [scr[1], bias]
        m_all = sb("m_all", [P, KD, T], offset=A1)
        c_sq = sb("c_sq", [P, KC, T], offset=A1)
        assert KC == 8
        s_hi = sb("s_hi", [P, KC, T], f32r, offset=A2)
        s_lo = sb("s_lo", [P, KC, T], f32r, offset=A2 + 4 * KC * T)
        m_tmp = sb("m_tmp", [P, 2, T], offset=A2 + 8 * KC * T)
        m_tmp2 = sb("m_tmp2", [P, 2, T], offset=A2 + 8 * KC * T + 8 * T)
        sig_a = qT
        sig_g = kT
        assert A2 + 8 * KC * T + 16 * T <= at_q
        act_hi = sb("act_hi", [P, KFA, T], f32r, offset=at_h_hi)
        act_lo = sb("act_lo", [P, KFA, T], f32r, offset=A0 + 4 * KFA * T)
        place[0] = A0 + 8 * KFA * T
        silu_g = sb("silu_g", [P, 2, T])
        act_f = sb("act_f", [P, 2, T])
        sq = sb("sq", [P, 2, T])
        ssq = sb("ssq", [P, T])
        rstd = sb("rstd", [P, T])
        var = sb("var", [P, T])
        end_ffn = place[0]
        ln_rstd = sb("ln_rstd", [P, T], offset=at_cur + 1536)
        ln_var = sb("ln_var", [P, T], offset=at_cur)
        y_tok = sb("y_tok", [P, 3, D], offset=A0)
        y_c = act_f
        assert max(end_attention, end_ffn) <= nc.sbuf_usable_end, (end_attention, end_ffn, nc.sbuf_usable_end)

        M = [ctx.enter_context(nc.psum_tensor(f"M{n}", [P, 512], f32)) for n in range(4)]
        T0, T1, S0, S1 = (ctx.enter_context(nc.psum_tensor(n, [P, 512], f32)) for n in ("T0", "T1", "S0", "S1"))
        SET = [M[0:2], M[2:4]]
        X_BANKS = (*M, T0, T1, S0, S1)
        XS_BANKS = (M[2], M[3], T0, M[1], S1, S0)
        NXS = len(XS_BANKS)
        IDX_BANKS = ((S0, S1), (T0, T1))
        IDX_AT = ((0, 1), (2,), (3,))

        def sem(name):
            return ctx.enter_context(nc.semaphore(name))

        x_in = [sem(f"x_in{t}") for t in range(3)]
        rows_in, conv_in, idx_in = sem("rows_in"), sem("conv_in"), sem("idx_in")
        raw_full = [sem(f"raw_full{s}") for s in range(4)]
        hi_ready, lo_ready = sem("hi_ready"), sem("lo_ready")
        units_used = sem("units_used")
        first_done = sem("first_done")
        act_evac, dve_evac = sem("act_evac"), sem("dve_evac")
        consts, pads = sem("consts"), sem("pads")
        rows_T, conv_T, cache_T, x_T = sem("rows_T"), sem("conv_T"), sem("cache_T"), sem("x_T")
        vecs_ready, convw_ready, x_evac = sem("vecs_ready"), sem("convw_ready"), sem("x_evac")
        x_tail_evac, x_std, rstd_ready = sem("x_tail_evac"), sem("x_std"), sem("rstd_ready")
        x_scaled_dve, x_scaled_act, xs_T = sem("x_scaled_dve"), sem("x_scaled_act"), sem("xs_T")
        h_hi_ready, h_ready = sem("h_hi_ready"), sem("h_ready")
        kiw_T, ki_var, ki_std, ki_done, kiT_done, kiT_ready = (
            sem(n) for n in ("kiw_T", "ki_var", "ki_std", "ki_done", "kiT_done", "kiT_ready"))
        idx_scored, relu_done, score_added = sem("idx_scored"), sem("relu_done"), sem("score_added")
        conv_tail_T, conv_rows_ready, conv_tail_out = (
            sem(n) for n in ("conv_tail_T", "conv_rows_ready", "conv_tail_out"))
        ck_full, cv_full, kv_out, kv_stored = (sem(n) for n in ("ck_full", "cv_full", "kv_out", "kv_stored"))
        ck_T_done, scores_done, v_T_done, k_T_done = (
            sem(n) for n in ("ck_T_done", "scores_done", "v_T_done", "k_T_done"))
        pT_done, pv_done, t_evac = sem("pT_done"), sem("pv_done"), sem("t_evac")
        scored, exp_done, rec_ready, p_ready = sem("scored"), sem("exp_done"), sem("rec_ready"), sem("p_ready")
        o_hi_done, o_lo_done = sem("o_hi_done"), sem("o_lo_done")
        conv_done, conv_summed, mean_done, centred, squared = (
            sem(n) for n in ("conv_done", "conv_summed", "mean_done", "centred", "squared"))
        var_done, ln_std, s_scaled, s_f_ready, s_hi_ready, s_ready = (
            sem(n) for n in ("var_done", "ln_std", "s_scaled", "s_f_ready", "s_hi_ready", "s_ready"))
        x_squared, ssq_added, ssq_sum, norm_std, m_done, h2_hi_ready, h2_ready = (
            sem(n) for n in ("x_squared", "ssq_added", "ssq_sum", "norm_std", "m_done", "h2_hi_ready", "h2_ready"))
        act_hi_ready, act_lo_ready = sem("act_hi_ready"), sem("act_lo_ready")
        silu_done, y_ready, y_T, y_evac, y_sum, y_std, y_rstd, y_scaled, y_scaled_act, y_out = (
            sem(n) for n in ("silu_done", "y_ready", "y_T", "y_evac", "y_sum", "y_std", "y_rstd", "y_scaled",
                             "y_scaled_act", "y_out"))
        dve_step, act_step, small_out = sem("dve_step"), sem("act_step"), sem("small_out")

        block = ctx.enter_context(nc.Block())

        SILU_AT, S_HI_AT = {8: (0, 1, 2, 3), 9: (4, 5), 10: (6, 7)}, (9, 11)
        HALVES = (slice(0, D // 2), slice(D // 2, D))
        HEAD_STEPS = ("cached keys", "scores 0", "scores 1", "values", "keys", "probs 0", "out 0", "probs 1", "out 1")

        @block.sync
        def _(sp):
            for t in range(2):
                sp.dma_start(x_tok[:, t, :], a["x_prompt"][0, t * P:(t + 1) * P, :]).then_inc(x_in[t], 16)
            sp.dma_start(x_tok[0:TS, 2, :], a["x_sample"][0]).then_inc(x_in[2], 16)

            def load(ph, i, u, w, k, col, n=NU, also_next=False, waited=False):
                s = u % 4
                if ph.freed(i, u) is not None and not waited:
                    sp.wait_ge(lo_ready, ph.freed(i, u + also_next))
                dst = w_raw[:, s, 0:KU * n].rearrange("p (t n) -> p t n", n=n)
                src = w[k * P:(k + KU) * P, :].rearrange("(t p) n -> p t n", p=P)[:, :, ds(col, n)]
                sp.dma_start(dst, src).then_inc(raw_full[s], 16)

            for u in range(KD // KU):
                load(W_KI, 0, u, w_in, KU * u, C_KI, NKI)
            with sp.Fori(0, W_QI.loops) as i:
                for u in range(4):
                    load(W_QI, i, u, w_in, KU * u, i * NU + C_QI)
            with sp.Fori(1, W_CONV.loops + 1) as j:
                i = j - 1
                for u in range(8):
                    load(W_CONV, i, u, w_in, KU * (u % 4), i * NU + (C_B, C_A)[u // 4], also_next=u == 3, waited=u == 4)
            with sp.Fori(0, W_HEAD.loops) as i:
                for u in range(12):
                    load(W_HEAD, i, u, w_in, KU * (u % 4), i * NU + (C_Q, C_K, C_V)[u // 4])
            with sp.Fori(1, W_MERGE.loops + 1) as j:
                i = j - 1
                for u in range(14):
                    w, c = ((w_in, C_GA), (w_in, C_GB), (w_attn_out, 0), (w_conv_out, 0))[u // 4]
                    load(W_MERGE, i, u, w, KU * (u % 4), i * NU + c, also_next=u == 7, waited=u == 8)
            with sp.Fori(1, W_OUT.loops + 1) as j:
                i = j - 1
                for u in range(8):
                    load(W_OUT, i, u, w_out, KU * (u % 4), i * (2 * NU) + NU * (u // 4))
            for up, down, k0, nk in ((W_UPA, W_DNA, 0, KFA), (W_UPB, W_DNB, KFA, KFB)):
                with sp.Fori(1, up.loops + 1) as j:
                    i = j - 1
                    for u in range(8):
                        load(up, i, u, (w_gate, w_up)[u // 4], KU * (u % 4), i * NU + k0 * P)
                with sp.Fori(1, down.loops + 1) as j:
                    i = j - 1
                    for u in range(nk // KU):
                        load(down, i, u, w_down, k0 + KU * u, i * NU)
            for h, c in enumerate(HALVES):
                sp.wait_ge(y_scaled, h + 1)
                sp.dma_start(o["y_prompt"][0, 0:P, c], y_tok[:, 0, c]).then_inc(y_out, 16)
                sp.wait_ge(y_scaled_act, h + 1)
                sp.dma_start(o["y_prompt"][0, P:TP, c], y_tok[:, 1, c]).then_inc(y_out, 16)
            for h, c in enumerate(HALVES):
                sp.wait_ge(y_scaled, h + 3)
                sp.dma_start(o["y_sample"][0, :, c], y_tok[0:TS, 2, c]).then_inc(y_out, 16)
            sp.wait_ge(y_out, 96)

        @block.gpsimd
        def _(pool):
            pool.sem_inc(kv_stored, 1)
            nc.gpsimd.memset(ident[:], 0.0).then_inc(consts, 1)
            nc.gpsimd.memset(ones[:], 1.0).then_inc(consts, 1)
            nc.gpsimd.memset(eps[:], EPS).then_inc(consts, 1)
            pool.wait_ge(consts, 3)
            nc.gpsimd.affine_select(out=ident[:], in_=ident[:], compare_op=ALU.not_equal, fill=1.0, base=0,
                                    pattern=[[-1, P]], channel_multiplier=1).then_inc(consts, 1)
            at_row = 0
            for name in ("g_mix", "g_ffn", "g_final", "conv_b", "conv_ln_g", "conv_ln_b"):
                v = a[name] if name == "g_final" else a[name][0]
                v = v.rearrange("(r c) -> r c", c=P)
                pool.dma_start(rows[at_row:at_row + v.shape[0], :], v).then_inc(rows_in, 16)
                at_row += v.shape[0]
            pool.dma_start(conv_w_rows[:], a["conv_w"][0]).then_inc(conv_in, 16)
            pool.dma_start(cache_rows[:], a["cache_conv"][0, 0]).then_inc(conv_in, 16)
            pool.dma_start(idx_g[:], a["idx_ln_g"][0].partition_broadcast(P)).then_inc(idx_in, 16)
            pool.dma_start(idx_b[:], a["idx_ln_b"][0].partition_broadcast(P)).then_inc(idx_in, 16)
            pool.wait_ge(h_ready, KD)
            nc.gpsimd.memset(u_all[:, :, 0:PAD], 0.0).then_inc(pads, 1)
            cki = a["cache_kidx"][0, 0].rearrange("(t p) d -> p t d", p=P)
            pool.dma_start(cki_tok[:, :, 0:DI], cki).then_inc(idx_in, 16)
            pool.dma_start(cki_tok[:, :, DI:2 * DI], cki).then_inc(idx_in, 16)
            pool.wait_ge(ki_done, 2)
            pool.dma_start(o["kidx_p"][0, 0].rearrange("(t p) d -> p t d", p=P),
                           ki_tok[:, 0:2, 0:DI]).then_inc(small_out, 16)
            pool.dma_start(o["kidx_s"][0, 0], ki_tok[0:TS, 2, 0:DI]).then_inc(small_out, 16)

            ck_v = a["cache_k"][0, 0].rearrange("(t p) h d -> p t (h d)", p=P)
            cv_v = a["cache_v"][0, 0].rearrange("(t p) h d -> p t (h d)", p=P)
            outs = [(o["k_p"], o["k_s"], k_tok), (o["v_p"], o["v_s"], v_tok)]

            def load_cached(p):
                pool.dma_start(ck_tok[:], ck_v[:, :, ds(p * NU, NU)]).then_inc(ck_full, 16)
                pool.dma_start(cv_tok[:], cv_v[:, :, ds(p * NU, NU)]).then_inc(cv_full, 16)

            def store_kv(p):
                pool.wait_ge(t_evac, 9 * p + 5)
                for prompt, sample, tok in outs:
                    pool.dma_start(prompt[0, 0].rearrange("(t p) h d -> p t (h d)", p=P)[:, :, ds(p * NU, NU)],
                                   tok[:, 0:2, :]).then_inc(kv_out, 16)
                    pool.dma_start(sample[0, 0].rearrange("t h d -> t (h d)")[:, ds(p * NU, NU)],
                                   tok[0:TS, 2, :]).then_inc(kv_out, 16)

            pool.wait_ge(small_out, 32)
            pool.wait_ge(dve_evac, at(DVE_EV, W_HEAD, 0, 0))
            pool.wait_ge(score_added, HI + 2)
            load_cached(0)
            pool.wait_ge(conv_rows_ready, 4)
            pool.dma_start(o["conv_p"][0, 0], conv_rows_out[:, 0, :]).then_inc(conv_tail_out, 16)
            pool.dma_start(o["conv_s"][0, 0], conv_rows_out[:, 1, :]).then_inc(conv_tail_out, 16)
            with pool.Fori(0, PAIRS - 1) as p:
                store_kv(p)
                pool.wait_ge(pv_done, 2 * p + 3)
                load_cached(p + 1)
                pool.wait_ge(kv_out, 64 * p + 64)
                pool.sem_inc(kv_stored, 1)
            for q in range(2):
                pool.wait_ge(centred, KC // 2 * (q + 1))
                c = slice(KC // 2 * q, KC // 2 * (q + 1))
                nc.gpsimd.tensor_tensor(c_sq[:, c, :], c_all[:, c, :], c_all[:, c, :], ALU.mult).then_inc(squared, 1)
            for n, half in enumerate((4, 2, 1)):
                pool.wait_ge(squared, n + 2)
                nc.gpsimd.tensor_tensor(c_sq[:, 0:half, :], c_sq[:, 0:half, :], c_sq[:, half:2 * half, :], ALU.add)\
                    .then_inc(squared, 1)
            store_kv(PAIRS - 1)
            pool.wait_ge(kv_out, 64 * PAIRS)
            pool.sem_inc(kv_stored, 1)
            pool.wait_ge(conv_tail_out, 32)

        @block.tensor
        def _(pe):
            mm, tr = nc.tensor.matmul, nc.tensor.transpose
            TOK = [(0, 0, P), (1, P, P), (2, TP, TS)]

            def unit(ph, i, u, k0, first, last, banks, hi, lo, n=NU, free=None, part=None):
                s = u % 4
                pe.wait_ge(hi_ready, ph.count(i, u))
                pe.wait_ge(lo_ready, ph.count(i, u))
                if part is not None:
                    pe.wait_ge(*part)
                tiles = [(b, b * P, min(P, n - b * P)) for b in range((n + P - 1) // P)]
                for b, c, m in tiles:
                    if first and free is not None:
                        pe.wait_ge(free[0], free[1](b))
                    for kk in range(KU):
                        wc = kk * n + c
                        start, stop = first and kk == 0, last and kk == KU - 1
                        x_hi, x_lo = hi[:, k0 + kk, :], lo[:, k0 + kk, :]
                        out = banks[b][0:m, 0:T]
                        mm(out, w_hi[:, s, wc:wc + m], x_hi, start=start, stop=False)
                        mm(out, w_hi[:, s, wc:wc + m], x_lo, start=False, stop=False)
                        done = mm(out, w_lo[:, s, wc:wc + m], x_hi, start=False, stop=stop)
                    if b == len(tiles) - 1:
                        done.then_inc(units_used, 1)
                    elif last:
                        done.then_inc(first_done, 1)

            pe.wait_ge(consts, 4)
            for t, c, n in TOK:
                pe.wait_ge(x_in[t], 16)
                per = 512 // n
                for q in range(KD // per):
                    if t == 2:
                        pe.wait_ge(x_evac, q + 1)
                    for j in range(per):
                        k = per * q + j
                        done = tr(X_BANKS[(4 * t + q) % 8][:, j * n:(j + 1) * n], x_tok[0:n, t, k * P:(k + 1) * P],
                                  ident[0:n, 0:n])
                    done.then_inc(x_T, 1)
            pe.wait_ge(x_evac, 8)
            pe.wait_ge(rows_in, 96)
            tr(S0[:, 0:NV], rows[:], ident[0:NV, 0:NV]).then_inc(rows_T, 1)
            pe.wait_ge(conv_in, 32)
            for c in range(KC):
                done = tr(S1[:, c * TAPS:(c + 1) * TAPS], conv_w_rows[:, c * P:(c + 1) * P], ident[0:TAPS, 0:TAPS])
            done.then_inc(conv_T, 1)
            for c in range(KC):
                done = tr(T1[:, c * PAD:(c + 1) * PAD], cache_rows[:, c * P:(c + 1) * P], ident[0:PAD, 0:PAD])
            done.then_inc(cache_T, 1)

            def scaled_tile(k):
                if k >= NXS:
                    pe.wait_ge(h_ready, k - NXS + 1)
                elif k == 4:
                    pe.wait_ge(convw_ready, 1)
                elif k == 5:
                    pe.wait_ge(vecs_ready, 1)
                for t, c, n in TOK:
                    done = tr(XS_BANKS[k % NXS][:, c:c + n], x_scaled[0:n, t, k * P:(k + 1) * P], ident[0:n, 0:n])
                done.then_inc(xs_T, 1)

            pe.wait_ge(x_tail_evac, 2)
            pe.wait_ge(x_scaled_dve, 2)
            pe.wait_ge(x_scaled_act, 1)
            for k in range(9):
                scaled_tile(k)
            for u in range(4):
                unit(W_KI, 0, u, KU * u, u == 0, u == 3, [M[0]], h_hi, h_lo, n=NKI, part=(h_ready, 4 * (u + 1)))
                for k in range(4 * u + 9, min(4 * u + 13, KD)):
                    scaled_tile(k)

            def score_index_head(p, hh):
                r = slice(DI * (hh % 2), DI * (hh % 2) + DI)
                q = qiT[r, hh // 2, :]
                bank0, bank1 = IDX_BANKS[hh % 2]
                pe.wait_ge(relu_done, 4 * p + (hh + 1))
                mm(bank0[:, 0:P], q[:, 0:P], kiT[r, 0:P], start=True, stop=True)
                mm(bank0[:, P:P + TP], q[:, P:TP], kiT[r, 0:TP], start=True, stop=True)
                mm(bank1[0:TS, 0:SK], q[:, TP:T], kiT[r, TP:TP + SK], start=True, stop=True).then_inc(idx_scored, 1)

            for u in range(4):
                unit(W_QI, 0, u, KU * u, u == 0, u == 3, SET[1], h_hi, h_lo)
                if u == 0:
                    pe.wait_ge(act_evac, 1)
                    for t, c, n in TOK:
                        done = tr(T0[0:n, t * NKI:(t + 1) * NKI], kiw[0:NKI, c:c + n], ident[0:NKI, 0:NKI])
                    done.then_inc(kiw_T, 1)
            pe.wait_ge(idx_in, 64)
            pe.wait_ge(ki_done, 2)
            for t in range(2):
                tr(T1[:, t * P:(t + 1) * P], ki_tok[:, t, :], ident[:])
                tr(T0[:, t * P:(t + 1) * P], cki_tok[:, t, :], ident[:])
            tr(T0[:, PAST:SK], ki_tok[0:TS, 2, :], ident[0:TS, 0:TS]).then_inc(kiT_done, 1)
            with pe.Fori(1, W_QI.loops) as i:
                for u in range(4):
                    unit(W_QI, i, u, KU * u, u == 0, u == 3, SET[1], h_hi, h_lo,
                         free=(act_evac, lambda b: at(ACT_EV, W_QI, i, b - 1)))
                    if u == 0:
                        pe.wait_ge(kiT_ready, 2)
                        pe.wait_ge(act_evac, at(ACT_EV, W_QI, i, 0))
                    for hh in IDX_AT[u] if u < 3 else ():
                        score_index_head(i - 1, hh)

            def conv_units(i, tail=None):
                for u in range(8):
                    g = u // 4
                    free = None
                    if not isinstance(i, int):
                        free = ((act_evac, lambda b: at(ACT_EV, W_CONV, i, b - 1)),
                                (dve_evac, lambda b: at(DVE_EV, W_CONV, i, b - 1)))[g]
                    if isinstance(i, int) and u == 4:
                        pe.wait_ge(act_evac, at(ACT_EV, W_CONV, 0, 0))
                    unit(W_CONV, i, u, KU * (u % 4), u % 4 == 0, u % 4 == 3, SET[g], h_hi, h_lo, free=free)
                    if tail is not None:
                        tail(u)

            def last_index_heads(u):
                if u == 0:
                    pe.wait_ge(act_evac, at(ACT_EV, W_CONV, 0, 0))
                for hh in IDX_AT[u] if u < 3 else ():
                    score_index_head(W_QI.loops - 1, hh)

            conv_units(0, last_index_heads)
            with pe.Fori(1, W_CONV.loops) as i:
                conv_units(i)
            pe.wait_ge(act_evac, at(ACT_EV, W_HEAD, 0, 0))

            def attend(p, step):
                hh = step in ("scores 1", "probs 1", "out 1")
                b = scr[int(hh)]
                if step == "cached keys":
                    pe.wait_ge(ck_full, 16 * p + 16)
                    pe.wait_ge(o_lo_done, 2 * p + 1)
                    for h in range(2):
                        for t in range(2):
                            done = tr(T0[:, (2 * h + t) * P:(2 * h + t + 1) * P], ck_tok[:, t, h * P:(h + 1) * P],
                                      ident[:])
                    done.then_inc(ck_T_done, 1)
                elif step in ("scores 0", "scores 1"):
                    h = int(hh)
                    pe.wait_ge(t_evac, 9 * p + 1)
                    pe.wait_ge(scored, 2 * p + h + 1)
                    mm(S0[:, 0:P], qT[:, h, 0:P], kT[:, h, 0:P], start=True, stop=True)
                    mm(S0[:, P:P + TP], qT[:, h, P:TP], kT[:, h, 0:TP], start=True, stop=True)
                    mm(S1[0:TS, 0:PAST], qT[:, h, TP:T], ck_T[:, h, :], start=True, stop=True)
                    mm(S1[0:TS, PAST:SK], qT[:, h, TP:T], kT[:, h, TP:T], start=True, stop=True)\
                        .then_inc(scores_done, 1)
                elif step in ("values", "keys"):
                    src, sig, k = (vT, v_T_done, 1) if step == "values" else (kT, k_T_done, 3)
                    pe.wait_ge(t_evac, 9 * p + k)
                    for t in range(2):
                        for h in range(2):
                            done = tr(T1[:, t * NU + h * P:t * NU + (h + 1) * P], src[:, h, t * P:(t + 1) * P],
                                      ident[:])
                    done.then_inc(sig, 1)
                    for h in range(2):
                        done = tr(T0[0:TS, h * P:(h + 1) * P], src[:, h, TP:T], ident[:])
                    done.then_inc(sig, 1)
                elif step in ("probs 0", "probs 1"):
                    pe.wait_ge(p_ready, 2 * p + hh + 1)
                    pe.wait_ge(t_evac, 9 * p + (7 if hh else 5))
                    pe.wait_ge(o_lo_done, 2 * p + hh + 1)
                    tr(T1[:, 0:P], b[:, 0:P], ident[:])
                    tr(T1[:, P:2 * P], b[:, P:2 * P], ident[:])
                    tr(T1[:, 2 * P:3 * P], b[:, 2 * P:3 * P], ident[:]).then_inc(pT_done, 1)
                    c0 = P + TP
                    tr(T0[:, 0:TS], b[0:TS, c0:c0 + P], ident[0:TS, 0:TS])
                    tr(T0[:, TS:2 * TS], b[0:TS, c0 + P:c0 + 2 * P], ident[0:TS, 0:TS])
                    tr(T0[0:TS, 2 * TS:3 * TS], b[0:TS, c0 + 2 * P:c0 + SK], ident[0:TS, 0:TS]).then_inc(pT_done, 1)
                else:
                    h = int(hh)
                    pe.wait_ge(t_evac, 9 * p + (9 if h else 7))
                    pe.wait_ge(cv_full, 16 * p + 16)
                    pe.wait_ge(o_lo_done, 2 * p + h + 1)
                    hc = slice(h * P, (h + 1) * P)
                    out = T0[:, 3 * TS:3 * TS + T]
                    mm(out[:, 0:TP], v_tok[:, 0, hc], pT[:, 0:TP], start=True, stop=False)
                    mm(out[:, P:TP], v_tok[:, 1, hc], pT[:, TP:TP + P], start=False, stop=True)
                    c0 = TP + P
                    mm(out[:, TP:T], cv_tok[:, 0, hc], pT[:, c0:c0 + TS], start=True, stop=False)
                    mm(out[:, TP:T], cv_tok[:, 1, hc], pT[:, c0 + TS:c0 + 2 * TS], start=False, stop=False)
                    mm(out[:, TP:T], v_tok[0:TS, 2, hc], pT[0:TS, c0 + 2 * TS:c0 + 3 * TS], start=False, stop=True)\
                        .then_inc(pv_done, 1)

            pe.sem_inc(pv_done, 1)

            def head_units(i, extra):
                for u in range(12):
                    g = u // 4
                    free = None
                    if g == 0 and not isinstance(i, int):
                        free = (act_evac, lambda b: at(ACT_EV, W_HEAD, i, b - 1))
                    if g == 1 and isinstance(i, int):
                        free = (dve_evac, lambda b: at(DVE_EV, W_HEAD, 0, b - 1))
                    if g == 2:
                        free = (act_evac, lambda b: at(ACT_EV, W_HEAD, i, b + 1))
                    unit(W_HEAD, i, u, KU * (u % 4), u % 4 == 0, u % 4 == 3, SET[g % 2], h_hi, h_lo, free=free)
                    extra(u)

            def conv_tail(u):
                if u == 0:
                    pe.wait_ge(dve_evac, at(DVE_EV, W_HEAD, 0, 0))
                if u < 2:
                    c0 = (TP, UW - PAD)[u]
                    for c in range(KC):
                        bank = ((T0, T1), (S0, S1))[u][c // 4]
                        done = tr(bank[0:PAD, (c % 4) * P:(c % 4 + 1) * P], u_all[:, c, c0:c0 + PAD], ident[:])
                        if c % 4 == 3:
                            done.then_inc(conv_tail_T, 1)

            head_units(0, conv_tail)
            pe.wait_ge(conv_rows_ready, 4)
            with pe.Fori(1, PAIRS) as i:
                def extra(u):
                    if u < len(HEAD_STEPS):
                        if u == 1:
                            pe.wait_ge(act_evac, at(ACT_EV, W_HEAD, i, 0))
                        attend(i - 1, HEAD_STEPS[u])
                head_units(i, extra)

            def merge_units(i, extra=None):
                for u in range(14):
                    g = u // 4
                    free = None
                    if g < 2 and not isinstance(i, int):
                        free = (dve_evac, lambda b: at(DVE_EV, W_MERGE, i, 2 * g + b - 3))
                    if g == 0 and isinstance(i, int):
                        free = (act_evac, lambda b: at(ACT_EV, W_MERGE, 0, b - 1))
                    if g == 1 and isinstance(i, int) and u == 4:
                        pe.wait_ge(centred, 1)
                    if g >= 2:
                        free = (act_evac, lambda b: at(ACT_EV, W_MERGE, i, 2 * (g - 2) + b + 1))
                    hi, lo = ((h_hi, h_lo), (h_hi, h_lo), (o_hi, o_lo), (s_hi, s_lo))[g]
                    part = (o_lo_done, H + 1) if u == 11 else (s_ready, u - 11) if u >= 12 else None
                    last = u in (3, 7, 11, 13)
                    unit(W_MERGE, i, u, KU * (u % 4), u % 4 == 0, last, SET[g % 2], hi, lo, free=free, part=part)
                    if extra is not None:
                        extra(u)

            def last_pair_and_norm(u):
                if u < 6:
                    attend(PAIRS - 1, HEAD_STEPS[u])
                if u == 0:
                    pe.wait_ge(act_evac, at(ACT_EV, W_MERGE, 0, 0))
                    pe.wait_ge(conv_summed, KC + 1)
                    mm(M[2][:, 0:T], ones[:], c_sum[:], start=True, stop=True).then_inc(mean_done, 1)
                if u == 5:
                    pe.wait_ge(squared, 5)
                    pe.wait_ge(scored, H + 1)
                    mm(S0[:, 0:T], ones[:], c_sq[:, 0, :], start=True, stop=True).then_inc(var_done, 1)
                if 5 <= u < 8:
                    attend(PAIRS - 1, HEAD_STEPS[u + 1])

            merge_units(0, last_pair_and_norm)
            with pe.Fori(1, W_MERGE.loops) as i:
                merge_units(i)

            with pe.Fori(0, W_OUT.loops) as i:
                for u in range(8):
                    g = u // 4
                    unit(W_OUT, i, u, KU * (u % 4), u % 4 == 0, u % 4 == 3, SET[g], h_hi, h_lo,
                         free=(dve_evac, lambda b: at(DVE_EV, W_OUT, i, 2 * g + b - 3)),
                         part=(h_ready, KD + u + 1) if g == 0 else None)

            def up_units(up, i, extra=None):
                for u in range(8):
                    g = u // 4
                    unit(up, i, u, KU * (u % 4), u % 4 == 0, u % 4 == 3, SET[g], o_hi, o_lo,
                         free=(dve_evac, lambda b: at(DVE_EV, up, i, 2 * g + b - 3)),
                         part=(h2_ready, KU * (u + 1)) if g == 0 else None)
                    if extra is not None:
                        extra(u)

            def sum_squares(u):
                if u == 1:
                    pe.wait_ge(ssq_added, KD + 2)
                    mm(T0[:, 0:T], ones[:], ssq[:], start=True, stop=True).then_inc(ssq_sum, 1)

            def down_unit(down, i, u, k0, n):
                unit(down, i, u, KU * u, u == 0, u == n - 1, (T0, T1), act_hi, act_lo,
                     free=(dve_evac, lambda b: at(DVE_EV, down, i, b - 1)), part=(act_lo_ready, k0 + KU * (u + 1)))

            up_units(W_UPA, 0, sum_squares)
            with pe.Fori(1, W_UPA.loops) as i:
                up_units(W_UPA, i)
            with pe.Fori(0, W_DNA.loops) as i:
                for u in range(KFA // KU):
                    down_unit(W_DNA, i, u, 0, KFA // KU)
            with pe.Fori(0, W_UPB.loops) as i:
                up_units(W_UPB, i)

            def result_by_token(i):
                for b in range(2):
                    pe.wait_ge(y_ready, 2 * i + (b + 1))
                    pe.wait_ge(y_evac, 2 * i + (b + 1))
                    for t, c, n in TOK:
                        done = tr((S0, S1)[b][0:n, t * P:(t + 1) * P], y_c[:, b, c:c + n], ident[:])
                    done.then_inc(y_T, 1)

            nb = KFB // KU
            for u in range(nb):
                down_unit(W_DNB, 0, u, KFA, nb)
            with pe.Fori(1, W_DNB.loops) as i:
                for u in range(nb):
                    down_unit(W_DNB, i, u, KFA, nb)
                    if u == 0:
                        result_by_token(i - 1)
            pe.wait_ge(ssq_added, 2 * KD)
            pe.wait_ge(dve_evac, at(DVE_EV, W_DNB, W_DNB.loops, 0))
            pe.wait_ge(x_squared, 2 * KD)
            for t, c, n in TOK:
                mm(T0[0:n, t:t + 1], ssq[:, c:c + n], ones[:, 0:1], start=True, stop=False)
                mm(T0[0:n, t:t + 1], sq[:, 0, c:c + n], ones[:, 0:1], start=False, stop=False)
                done = mm(T0[0:n, t:t + 1], sq[:, 1, c:c + n], ones[:, 0:1], start=False, stop=True)
            done.then_inc(y_sum, 1)
            result_by_token(W_DNB.loops - 1)

        @block.scalar
        def _(act):
            act_fn = nc.scalar.activation
            step = Steps()
            act.sem_inc(relu_done, 2)
            act.sem_inc(y_evac, 2)

            def high_half(ph, i, u):
                if u >= ph.n:
                    i, u = i + 1, u - ph.n
                n = KU * NKI if ph is W_KI else KU * NU
                s = u % 4
                act.wait_ge(raw_full[s], 16 * ph.fills(i, u))
                if ph.freed(i, u) is not None:
                    act.wait_ge(units_used, ph.freed(i, u))
                act_fn(w_hi[:, s, 0:n], w_raw[:, s, 0:n], ACT.Copy).then_inc(hi_ready, 1)

            def group_tile(ph, i, u, g, b):
                if b == 0:
                    act.wait_ge(first_done, at(GROUPS, ph, i, g + 1))
                else:
                    act.wait_ge(units_used, ph.count(i, u))

            act.wait_ge(consts, 4)
            act_fn(stat_r[:, 0:1], eps[:], ACT.Sqrt).then_inc(act_step, 1)
            step.up()
            act.wait_ge(dve_step, 1)
            for t, n in ((0, P), (1, P), (2, TS)):
                act.wait_ge(act_step, step.now())
                act.wait_ge(x_in[t], 16)
                act_fn(junk[0:n, :], x_tok[0:n, t, :], ACT.Square, accum_out=stat[0:n, t:t + 1]).then_inc(act_step, 1)
                step.up()
            act.wait_ge(act_step, step.now())
            act_fn(stat_r[:], stat[:], ACT.Sqrt, bias=eps[:], scale=1.0 / D).then_inc(x_std, 1)
            for q in range(2):
                act.wait_ge(x_T, 9 + q)
                act_fn(xT[:, 8 * q:8 * q + 8, TP:T], M[q][:].rearrange("p (k n) -> p k n", n=TS), ACT.Copy)\
                    .then_inc(x_tail_evac, 1)
            high_half(W_KI, 0, 0)
            act.wait_ge(rstd_ready, 1)
            act_fn(x_scaled[:, 1, :], x_tok[:, 1, :], ACT.Copy, scale=stat_r[:, 1:2]).then_inc(x_scaled_act, 1)
            act.wait_ge(rows_T, 1)
            act_fn(vecs[:], S0[:, 0:NV], ACT.Copy).then_inc(vecs_ready, 1)
            act.wait_ge(vecs_ready, 1)

            for k in range(KD):
                act.wait_ge(xs_T, k + 1)
                act_fn(h_hi[:, k, :], XS_BANKS[k % NXS][:, 0:T], ACT.Copy, scale=G_MIX[:, k:k + 1])\
                    .then_inc(h_hi_ready, 1)
                if k % 4 == 3 and k < KD - 1:
                    high_half(W_KI, 0, k // 4 + 1)
                if k == KD - 2:
                    high_half(W_QI, 0, 0)
            high_half(W_QI, 0, 1)
            act.wait_ge(units_used, W_KI.count(0, 3))
            act_fn(kiw[0:NKI, :], M[0][0:NKI, 0:T], ACT.Copy).then_inc(act_evac, 1)

            def merged_high(q):
                act_fn(h_hi[:, 4 * q:4 * q + 4, :], m_all[:, 4 * q:4 * q + 4, :], ACT.Copy).then_inc(h_hi_ready, 1)

            def evac(ph, i, u, g, dst, fn, wait=None):
                for b in range(2):
                    group_tile(ph, i, u, g, b)
                    if wait is not None and b == 0:
                        act.wait_ge(*wait)
                    act_fn(dst[:, b, :], SET[BANK[ph][g]][b][:, 0:T], fn).then_inc(act_evac, 1)

            BANK = {W_QI: [1], W_CONV: [0, 1], W_HEAD: [0, 1, 0], W_MERGE: [0, 1, 0, 1], W_UPA: [0, 1], W_UPB: [0, 1]}

            def relu_head(p, hh):
                act.wait_ge(idx_scored, 4 * p + (hh + 1))
                act.wait_ge(score_added, 4 * p + (hh + 1))
                r = relu_sc[hh % 2]
                bank0, bank1 = IDX_BANKS[hh % 2]
                act_fn(r[0:TS, P + TP:SW], bank1[0:TS, 0:SK], ACT.Relu, scale=IDX_SCALE).then_inc(act_step, 1)
                act.wait_ge(act_step, step.up())
                act_fn(r[:, 0:P + TP], bank0[:, 0:P + TP], ACT.Relu, scale=IDX_SCALE).then_inc(relu_done, 1)

            for u in range(4):
                high_half(W_QI, 0, u + 2)
                if u == 0:
                    act.wait_ge(ki_var, 3)
                    act_fn(istd[:], mv[:, :, 1], ACT.Sqrt, bias=eps[:]).then_inc(ki_std, 1)
            evac(W_QI, 0, 3, 0, qiT, ACT.Copy)
            act.wait_ge(kiT_done, 1)
            act_fn(kiT[:, 0:TP], T1[:, 0:TP], ACT.Copy).then_inc(kiT_ready, 1)
            act_fn(kiT[:, TP:TP + SK], T0[:, 0:SK], ACT.Copy).then_inc(kiT_ready, 1)
            with act.Fori(1, W_QI.loops) as i:
                step.enter(i, 4, 1)
                for u in range(4):
                    high_half(W_QI, i, u + 2)
                    for hh in IDX_AT[u] if u < 3 else ():
                        relu_head(i - 1, hh)
                evac(W_QI, i, 3, 0, qiT, ACT.Copy)
                step.leave(W_QI.loops - 1)

            for i0 in (0, 1):
                loop = ExitStack()
                i = 0 if i0 == 0 else loop.enter_context(act.Fori(1, W_CONV.loops))
                for u in range(8):
                    high_half(W_CONV, i, u + 2)
                    for hh in IDX_AT[u] if i0 == 0 and u < 3 else ():
                        relu_head(W_QI.loops - 1, hh)
                    if u == 3:
                        evac(W_CONV, i, 3, 0, sig_b, ACT.Sigmoid,
                             None if i0 == 0 else (dve_evac, at(DVE_EV, W_CONV, i, 0)))
                loop.close()

            def probabilities(p, h):
                act.wait_ge(rec_ready, 2 * p + h + 1)
                act_fn(scr[h][:, 0:P], scr[h][:, 0:P], ACT.Copy, scale=srec[:, h, 0:1]).then_inc(act_step, 1)
                step.up()
                act_fn(scr[h][:, P:P + TP], scr[h][:, P:P + TP], ACT.Copy, scale=srec[:, h, 1:2])\
                    .then_inc(act_step, 1)
                act.wait_ge(act_step, step.up())
                act_fn(scr[h][0:TS, P + TP:SW], scr[h][0:TS, P + TP:SW], ACT.Copy, scale=srec[0:TS, h, 2:3])\
                    .then_inc(p_ready, 1)

            def attend(p, u):
                if u == 0:
                    act.wait_ge(ck_T_done, p + 1)
                    act_fn(ck_T[:].rearrange("p h t -> p (h t)"), T0[:, 0:2 * PAST], ACT.Copy).then_inc(t_evac, 1)
                if u == 2:
                    probabilities(p, 0)
                if u in (1, 2):
                    h = u - 1
                    act.wait_ge(scored, 2 * p + h + 2)
                    for t, c, n, w in ((0, 0, P, P), (1, P, P, TP), (2, P + TP, TS, SK)):
                        act_fn(scr[h][0:n, c:c + w], scr[h][0:n, c:c + w], ACT.Exp, bias=snmax[0:n, h, t:t + 1],
                               accum_out=ssum[0:n, h, t:t + 1]).then_inc(exp_done, 1)
                if u in (3, 4):
                    sig, tok = ((v_T_done, v_tok), (k_T_done, k_tok))[u - 3]
                    act.wait_ge(kv_stored, p + 1)
                    act.wait_ge(sig, 2 * p + 1)
                    act_fn(tok[:, 0:2, :].rearrange("p t c -> p (t c)"), T1[:, 0:2 * NU], ACT.Copy)\
                        .then_inc(t_evac, 1)
                    act.wait_ge(sig, 2 * p + 2)
                    act_fn(tok[0:TS, 2, :], T0[0:TS, 0:NU], ACT.Copy).then_inc(t_evac, 1)
                if u == 4:
                    probabilities(p, 1)
                if u in (5, 7):
                    h = (u - 5) // 2
                    act.wait_ge(pT_done, 4 * p + 2 * h + 1)
                    act.wait_ge(pv_done, 2 * p + h + 1)
                    act_fn(pT[:, 0:TP + P], T1[:, 0:TP + P], ACT.Copy).then_inc(t_evac, 1)
                    act.wait_ge(pT_done, 4 * p + 2 * h + 2)
                    act_fn(pT[:, TP + P:TP + P + 2 * TS], T0[:, 0:2 * TS], ACT.Copy).then_inc(act_step, 1)
                    step.up()
                    act_fn(pT[0:TS, TP + P + 2 * TS:PW], T0[0:TS, 2 * TS:3 * TS], ACT.Copy).then_inc(t_evac, 1)
                if u in (6, 8):
                    h = (u - 6) // 2
                    if h == 0:
                        act.wait_ge(conv_tail_out, 32)
                    act.wait_ge(pv_done, 2 * p + h + 2)
                    act_fn(o_hi[:, ds(2 * p + h, 1), :], T0[:, 3 * TS:3 * TS + T], ACT.Copy).then_inc(o_hi_done, 1)

            ATT_STEPS = 6

            for i0 in (0, 1):
                loop = ExitStack()
                i = 0 if i0 == 0 else loop.enter_context(act.Fori(1, PAIRS))
                if i0:
                    step.enter(i, ATT_STEPS, 1)
                for u in range(12):
                    high_half(W_HEAD, i, u + 2)
                    if i0:
                        attend(i - 1, u)
                    if i0 == 0 and u < 2:
                        for half, bank in enumerate(((T0, T1), (S0, S1))[u]):
                            act.wait_ge(conv_tail_T, 2 * u + half + 1)
                            act_fn(conv_rows_out[:, u, half * 512:(half + 1) * 512], bank[0:PAD, :], ACT.Copy)\
                                .then_inc(conv_rows_ready, 1)
                    if u % 4 == 3:
                        g = u // 4
                        wait = None
                        if i0:
                            wait = ((scores_done, 2 * i), (k_T_done, 2 * i), (v_T_done, 2 * i))[g]
                        evac(W_HEAD, i, u, g, (qT, kT, vT)[g], ACT.Copy, wait)
                if i0:
                    step.leave(PAIRS - 1)
                loop.close()

            last_merge = W_MERGE.loops - 1
            for i0 in (0, 1, 2):
                loop = ExitStack()
                i = (0, None, last_merge)[i0] if i0 != 1 else loop.enter_context(act.Fori(1, last_merge))
                for u in range(14):
                    if i0 == 0 and u == 5:
                        attend(PAIRS - 1, u)
                    high_half(W_MERGE, i, u + 2)
                    if i0 == 0 and u < 5:
                        attend(PAIRS - 1, u)
                    if i0 == 0 and 5 <= u < 8:
                        attend(PAIRS - 1, u + 1)
                    if i0 == 0 and u == 5:
                        act.wait_ge(var_done, 1)
                        act_fn(ln_rstd[:], S0[:, 0:T], ACT.Sqrt, bias=eps[:], scale=1.0 / DC).then_inc(ln_std, 1)
                    if i0 == 0 and u in S_HI_AT:
                        c = 4 * S_HI_AT.index(u)
                        act.wait_ge(s_f_ready, c + 4)
                        act.wait_ge(kv_stored, PAIRS + 1)
                        act_fn(s_hi[:, c:c + 4, :], c_all[:, c:c + 4, :], ACT.Copy).then_inc(s_hi_ready, 1)
                    for c in SILU_AT.get(u, ()) if i0 == 0 else ():
                        act.wait_ge(s_scaled, c + 1)
                        act_fn(c_all[:, c, :], c_all[:, c, :], ACT.Silu, bias=LN_B[:, c:c + 1],
                               scale=LN_G[:, c:c + 1]).then_inc(s_f_ready, 1)
                    if u in (3, 7):
                        g = u // 4
                        wait = None if i0 == 0 else (dve_evac, at(DVE_EV, W_MERGE, i, 0))
                        evac(W_MERGE, i, u, g, (sig_a, sig_g)[g], ACT.Sigmoid, wait)
                    if i0 == 2 and u in (9, 10, 11):
                        act.wait_ge(units_used, W_MERGE.count(i, 7))
                        act.wait_ge(m_done, 4 * (u - 8))
                        merged_high(u - 9)
                loop.close()
            high_half(W_OUT, 0, 2)
            act.wait_ge(m_done, KD)
            merged_high(3)

            def square(ph, i, b, k, n):
                act.wait_ge(dve_evac, at(DVE_EV, ph, i, n + 1))
                act.wait_ge(ssq_added, k + (1 if ph is W_OUT else KD + 1))
                act_fn(sq[:, b, :], xT[:, ds(k, 1), :], ACT.Square).then_inc(x_squared, 1)

            with act.Fori(0, W_OUT.loops) as i:
                for u in range(8):
                    if u:
                        high_half(W_OUT, i, u + 2)
                    if u % 4 == 3:
                        for b in range(2):
                            if u == 7 and b == 1:
                                high_half(W_OUT, i, 10)
                            n = 2 * (u // 4) + b
                            square(W_OUT, i, b, i * 4 + n, n)
                            act_fn(o_hi[:, ds(i * 4 + n, 1), :], xT[:, ds(i * 4 + n, 1), :], ACT.Copy,
                                   scale=G_FFN[:, ds(i * 4 + n, 1)]).then_inc(h2_hi_ready, 1)

            for up, down, nk, k0 in ((W_UPA, W_DNA, KFA, 0), (W_UPB, W_DNB, KFB, KFA)):
                for i0 in (0, 1):
                    if i0 == 0 and up is W_UPB:
                        continue
                    loop = ExitStack()
                    i = 0 if i0 == 0 else loop.enter_context(act.Fori(1 if up is W_UPA else 0, up.loops))
                    for u in range(8):
                        if i0 or u:
                            high_half(up, i, u + 2)
                        if i0 == 0 and u == 1:
                            act.wait_ge(ssq_sum, 1)
                            act_fn(rstd[:], T0[:, 0:T], ACT.Sqrt, bias=eps[:], scale=1.0 / D).then_inc(norm_std, 1)
                            act_fn(var[:], T0[:, 0:T], ACT.Copy, scale=1.0 / D, bias=EPS).then_inc(norm_std, 1)
                        if u == 3:
                            for b in range(2):
                                act.wait_ge(dve_evac, at(DVE_EV, up, i, b + 1))
                                act_fn(silu_g[:, b, :], silu_g[:, b, :], ACT.Silu).then_inc(silu_done, 1)
                        if u == 7:
                            for b in range(2):
                                act.wait_ge(dve_evac, at(DVE_EV, up, i, b + 3))
                                act_fn(act_hi[:, ds(i * 2 + b, 1), :], act_f[:, b, :], ACT.Copy)\
                                    .then_inc(act_hi_ready, 1)
                    loop.close()
                n = nk // KU
                if down is W_DNA:
                    with act.Fori(0, down.loops) as i:
                        for u in range(n):
                            high_half(down, i, u + 2)

            def result_rows(i):
                for b in range(2):
                    act.wait_ge(y_T, 2 * i + (b + 1))
                    bank = (S0, S1)[b]
                    act_fn(y_tok[:, 0:2, ds((2 * i + b) * P, P)], bank[:, 0:2 * P].rearrange("p (t c) -> p t c", c=P),
                           ACT.Copy).then_inc(act_step, 1)
                    step.up()
                    act_fn(y_tok[0:TS, 2, ds((2 * i + b) * P, P)], bank[0:TS, 2 * P:3 * P], ACT.Copy)\
                        .then_inc(y_evac, 1)

            for i0 in (0, 1, 2):
                loop = ExitStack()
                i = (0, None, W_DNB.loops - 1)[i0] if i0 != 1 else loop.enter_context(act.Fori(1, W_DNB.loops - 1))
                if i0 == 1:
                    step.enter(i, 2, 1)
                for u in range(n):
                    if i0 < 2 or u + 2 < n:
                        high_half(W_DNB, i, u + 2)
                    if i0 and u == 0:
                        result_rows(i - 1)
                if i0 == 2:
                    act_fn(stat_r[:, 0:1], eps[:], ACT.Sqrt).then_inc(act_step, 1)
                    act.wait_ge(act_step, step.up())
                for b in range(2):
                    square(W_DNB, i, b, 2 * i + b, b)
                if i0 == 1:
                    step.leave(W_DNB.loops - 2)
                loop.close()
            act.wait_ge(y_sum, 1)
            act_fn(stat_r[:, 0:2], T0[:, 0:2], ACT.Sqrt, bias=eps[:], scale=1.0 / D).then_inc(y_std, 1)
            act_fn(stat_r[0:TS, 2:3], T0[0:TS, 2:3], ACT.Sqrt, bias=eps[0:TS, :], scale=1.0 / D).then_inc(y_std, 1)
            result_rows(W_DNB.loops - 1)
            act.wait_ge(y_rstd, 1)
            act.wait_ge(act_step, step.now())
            for c in HALVES:
                act_fn(y_tok[:, 1, c], y_tok[:, 1, c], ACT.Copy, scale=stat_r[:, 1:2]).then_inc(y_scaled_act, 1)

        @block.vector
        def _(dve):
            v = nc.vector
            step = Steps()

            def low_half(ph, i, u):
                if u >= ph.n:
                    i, u = i + 1, u - ph.n
                n = KU * NKI if ph is W_KI else KU * NU
                s = u % 4
                dve.wait_ge(hi_ready, ph.count(i, u))
                v.tensor_tensor(w_lo[:, s, 0:n], w_raw[:, s, 0:n], w_hi[:, s, 0:n].bitcast(f32), ALU.subtract)\
                    .then_inc(lo_ready, 1)

            def group_tile(ph, i, u, g, b):
                if b == 0:
                    dve.wait_ge(first_done, at(GROUPS, ph, i, g + 1))
                else:
                    dve.wait_ge(units_used, ph.count(i, u))

            dve.sem_inc(scored, 1)
            dve.sem_inc(o_lo_done, 1)
            dve.sem_inc(ssq_added, 2)
            dve.sem_inc(score_added, 2)
            v.memset(stat[:], 1.0).then_inc(dve_step, 1)
            step.up()
            v.memset(mv[:], 1.0).then_inc(dve_step, 1)
            step.up()
            v.memset(bn[:], 0.0).then_inc(dve_step, 1)
            step.up()
            v.memset(score[:], 0.0).then_inc(dve_step, 1)
            step.up()

            def newton(r, v_, t):
                v.reciprocal(r, r).then_inc(dve_step, 1)
                dve.wait_ge(dve_step, step.up())
                v.tensor_tensor(t, r, r, ALU.mult).then_inc(dve_step, 1)
                dve.wait_ge(dve_step, step.up())
                v.tensor_tensor(t, t, v_, ALU.mult).then_inc(dve_step, 1)
                dve.wait_ge(dve_step, step.up())
                v.tensor_scalar(t, t, -0.5, 1.5, ALU.mult, ALU.add).then_inc(dve_step, 1)
                dve.wait_ge(dve_step, step.up())
                return v.tensor_tensor(r, r, t, ALU.mult)

            for t, c in ((0, 0), (1, P)):
                for q in range(4):
                    dve.wait_ge(x_T, 4 * t + q + 1)
                    v.tensor_copy(xT[:, 4 * q:4 * q + 4, c:c + P],
                                  X_BANKS[4 * t + q][:].rearrange("p (k n) -> p k n", n=P)).then_inc(x_evac, 1)
            dve.wait_ge(x_std, 1)
            v.tensor_scalar(stat_v[:], stat[:], 1.0 / D, EPS, ALU.mult, ALU.add).then_inc(dve_step, 1)
            step.up()
            newton(stat_r[:], stat_v[:], stat_t[:]).then_inc(rstd_ready, 1)
            dve.wait_ge(rstd_ready, 1)
            for t, n in ((0, P), (2, TS)):
                v.tensor_scalar(x_scaled[0:n, t, :], x_tok[0:n, t, :], stat_r[0:n, t:t + 1], None, ALU.mult)\
                    .then_inc(x_scaled_dve, 1)

            def merged_low(q):
                dve.wait_ge(h_hi_ready, KD + q + 1)
                v.tensor_tensor(h_lo[:, 4 * q:4 * q + 4, :], m_all[:, 4 * q:4 * q + 4, :],
                                h_hi[:, 4 * q:4 * q + 4, :].bitcast(f32), ALU.subtract).then_inc(h_ready, 1)

            dve.wait_ge(conv_T, 1)
            v.tensor_copy(conv_w[:, :, 0:TAPS], S1[:, 0:KC * TAPS].rearrange("p (c t) -> p c t", t=TAPS))\
                .then_inc(convw_ready, 1)

            low_half(W_KI, 0, 0)
            dve.wait_ge(vecs_ready, 1)
            for k in range(KD):
                dve.wait_ge(h_hi_ready, k + 1)
                v.scalar_tensor_tensor(out=h_lo[:, k, :], in0=XS_BANKS[k % NXS][:, 0:T], scalar=G_MIX[:, k:k + 1],
                                       in1=h_hi[:, k, :].bitcast(f32), op0=ALU.mult, op1=ALU.subtract)\
                    .then_inc(h_ready, 1)
                if k % 4 == 3 and k < KD - 1:
                    low_half(W_KI, 0, k // 4 + 1)
            low_half(W_QI, 0, 0)
            low_half(W_QI, 0, 1)
            v.tensor_copy(conv_w[:, :, TAPS:TAPS + 1], CONV_B.unsqueeze(2)).then_inc(dve_step, 1)
            step.up()
            dve.wait_ge(cache_T, 1)
            v.tensor_copy(u_all[:, :, PAD + TP:2 * PAD + TP],
                          T1[:, 0:KC * PAD].rearrange("p (c t) -> p c t", t=PAD)).then_inc(dve_step, 1)
            dve.wait_ge(dve_step, step.up())

            ROWS = ((0, P), (1, P), (2, TS))
            for u in range(4):
                low_half(W_QI, 0, u + 2)
                if u == 0:
                    dve.wait_ge(kiw_T, 1)
                    dve.wait_ge(idx_in, 64)
                    for t, n in ROWS:
                        v.bn_stats(bn[0:n, t, :], T0[0:n, t * NKI:t * NKI + DI]).then_inc(dve_step, 1)
                        dve.wait_ge(dve_step, step.up())
                    for t, n in ROWS:
                        v.bn_aggr(mv[0:n, t, :], bn[0:n, t, :]).then_inc(ki_var, 1)
                    for t, n in ROWS:
                        v.tensor_copy(w_tok[0:n, t, :], T0[0:n, t * NKI + DI:(t + 1) * NKI]).then_inc(dve_step, 1)
                        step.up()
                    dve.wait_ge(ki_std, 1)
                    v.tensor_scalar(stat_v[:], mv[:, :, 1], EPS, None, ALU.add).then_inc(dve_step, 1)
                    step.up()
                    newton(istd[:], stat_v[:], stat_t[:]).then_inc(dve_step, 1)
                    dve.wait_ge(dve_step, step.up())
                if u == 1:
                    for t, n in ROWS:
                        k = ki_tok[0:n, t, 0:DI]
                        v.tensor_scalar(k, T0[0:n, t * NKI:t * NKI + DI], mv[0:n, t, 0:1], istd[0:n, t:t + 1],
                                        ALU.subtract, ALU.mult).then_inc(dve_step, 1)
                        dve.wait_ge(dve_step, step.up())
                        v.tensor_tensor(k, k, idx_g[0:n, :], ALU.mult).then_inc(dve_step, 1)
                        dve.wait_ge(dve_step, step.up())
                        v.tensor_tensor(k, k, idx_b[0:n, :], ALU.add).then_inc(dve_step, 1)
                        dve.wait_ge(dve_step, step.up())
                    v.tensor_copy(ki_tok[:, 0:2, DI:2 * DI], ki_tok[:, 0:2, 0:DI]).then_inc(ki_done, 1)
                    v.tensor_copy(ki_tok[0:TS, 2, DI:2 * DI], ki_tok[0:TS, 2, 0:DI]).then_inc(ki_done, 1)

            SPAN = ((0, 0, P, P), (1, P, P, TP), (2, P + TP, TS, SK))

            def add_head(p, hh):
                if hh == 0:
                    dve.wait_ge(score_added, 4 * p + 2)
                    v.tensor_copy(w_grp[:, 0:2, :], w_tok[:, 0:2, ds(4 * p, 4)]).then_inc(dve_step, 1)
                    step.up()
                    v.tensor_copy(w_grp[0:TS, 2, :], w_tok[0:TS, 2, ds(4 * p, 4)]).then_inc(dve_step, 1)
                    dve.wait_ge(dve_step, step.up())
                dve.wait_ge(relu_done, 4 * p + (hh + 3))
                dve.wait_ge(score_added, 4 * p + (hh + 2))
                r = relu_sc[hh % 2]
                for t, c, n, w in SPAN:
                    done = v.scalar_tensor_tensor(out=score[0:n, c:c + w], in0=r[0:n, c:c + w],
                                                  scalar=w_grp[0:n, t, hh:hh + 1], in1=score[0:n, c:c + w],
                                                  op0=ALU.mult, op1=ALU.add)
                done.then_inc(score_added, 1)

            with dve.Fori(1, W_QI.loops) as i:
                step.enter(i, 2, 1)
                for u in range(4):
                    low_half(W_QI, i, u + 2)
                    for hh in IDX_AT[u] if u < 3 else ():
                        add_head(i - 1, hh)
                step.leave(W_QI.loops - 1)

            def top_round(todo):
                for t, c, n, w in todo:
                    v.max(top8[0:n, t, :], score[0:n, c:c + w]).then_inc(dve_step, 1)
                    step.up()
                for t, c, n, w in todo:
                    dve.wait_ge(dve_step, step.now() - (len(todo) - 1))
                    v.match_replace(score[0:n, c:c + w], top8[0:n, t, :], score[0:n, c:c + w], REMOVED)\
                        .then_inc(dve_step, 1)
                    step.up()
                dve.wait_ge(dve_step, step.now())

            last_conv = W_CONV.loops - 1
            ROUNDS_P, ROUNDS_S = TOP_P // 8 // (last_conv - 1), TOP_S // 8 // (last_conv - 1)
            assert ROUNDS_P * 8 * (last_conv - 1) == TOP_P and ROUNDS_S * 8 * (last_conv - 1) == TOP_S
            for i in range(W_CONV.loops):
                for u in range(8):
                    low_half(W_CONV, i, u + 2)
                    for hh in IDX_AT[u] if i == 0 and u < 3 else ():
                        add_head(W_QI.loops - 1, hh)
                    if i == 0 and u == 4:
                        dve.wait_ge(score_added, HI + 2)
                        v.memset(score[0:CHUNK, CHUNK:P], OUTSIDE).then_inc(dve_step, 1)
                        step.up()
                        v.memset(score[0:CHUNK, P + TP - CHUNK:P + TP], OUTSIDE).then_inc(dve_step, 1)
                        dve.wait_ge(dve_step, step.up())
                    if 0 < i < last_conv and u < ROUNDS_S:
                        top_round(SPAN if u < ROUNDS_P else SPAN[2:])
                    if i == last_conv and u == 0:
                        for t, c, n, w in SPAN:
                            v.tensor_scalar(bias[0:n, c:c + w], score[0:n, c:c + w], IS_REMOVED, BIG,
                                            ALU.is_gt, ALU.mult).then_inc(dve_step, 1)
                            step.up()
                        v.memset(smax[:], 0.0).then_inc(dve_step, 1)
                        dve.wait_ge(dve_step, step.up())
                for b in range(2):
                    dve.wait_ge(act_evac, at(ACT_EV, W_CONV, i, b + 1))
                    group_tile(W_CONV, i, 7, 1, b)
                    v.tensor_tensor(u_all[:, ds(2 * i + b, 1), PAD:PAD + TP], SET[1][b][:, 0:TP],
                                    sig_b[:, b, 0:TP], ALU.mult).then_inc(dve_step, 1)
                    step.up()
                    v.tensor_tensor(u_all[:, ds(2 * i + b, 1), 2 * PAD + TP:UW], SET[1][b][:, TP:T],
                                    sig_b[:, b, TP:T], ALU.mult).then_inc(dve_evac, 1)

            TAPS_AT = [3] * 9 + [2, 2, 0]
            assert sum(TAPS_AT) == TAPS

            def convolve(i, u):
                if u == 0:
                    v.tensor_copy(u_cur[:], u_all[:, ds(i, 1), :]).then_inc(dve_step, 1)
                    step.up()
                    v.tensor_copy(w_cur[:], conv_w[:, ds(i, 1), :]).then_inc(dve_step, 1)
                    dve.wait_ge(dve_step, step.up())
                first = sum(TAPS_AT[:u])
                for t in range(first, first + TAPS_AT[u]):
                    if t == 0:
                        v.tensor_scalar(acc[:], u_cur[:, 0:CW], w_cur[:, 0:1], w_cur[:, TAPS:TAPS + 1],
                                        ALU.mult, ALU.add).then_inc(dve_step, 1)
                    else:
                        v.scalar_tensor_tensor(out=acc[:], in0=u_cur[:, t:t + CW], scalar=w_cur[:, t:t + 1],
                                               in1=acc[:], op0=ALU.mult, op1=ALU.add).then_inc(dve_step, 1)
                    dve.wait_ge(dve_step, step.up())
                if u == 11:
                    v.tensor_copy(c_all[:, ds(i, 1), 0:TP], acc[:, 0:TP]).then_inc(dve_step, 1)
                    step.up()
                    v.tensor_copy(c_all[:, ds(i, 1), TP:T], acc[:, TP + PAD:CW]).then_inc(conv_done, 1)
                    dve.wait_ge(conv_done, i + 1)
                    dve.wait_ge(conv_summed, i + 1)
                    v.tensor_tensor(c_sum[:], c_sum[:], c_all[:, ds(i, 1), :], ALU.add).then_inc(conv_summed, 1)

            CONV_STEPS = 2 + TAPS + 1

            def attend(p, u):
                if u in (2, 3):
                    h = u - 2
                    dve.wait_ge(exp_done, 6 * p + 3 * h + 3)
                    v.reciprocal(srec[:, h, :], ssum[:, h, :]).then_inc(rec_ready, 1)
                if u in (1, 2):
                    h = u - 1
                    dve.wait_ge(scores_done, 2 * p + h + 1)
                    v.memset(ssum[:, h, :], 1.0).then_inc(dve_step, 1)
                    step.up()
                    for (t, c, n, w), bank in zip(SPAN, (S0[:, 0:P], S0[:, P:P + TP], S1[0:TS, 0:SK])):
                        v.tensor_tensor_reduce(out=scr[h][0:n, c:c + w], in0=bank, in1=bias[0:n, c:c + w], scale=SCALE,
                                               scalar=4 * BIG, op0=ALU.add, op1=ALU.max,
                                               accum_out=smax[0:n, h, t:t + 1]).then_inc(dve_step, 1)
                        done = step.up()
                    dve.wait_ge(dve_step, done)
                    v.tensor_scalar(snmax[:, h, :], smax[:, h, :], -1.0, None, ALU.mult).then_inc(scored, 1)
                if u in (6, 8):
                    h = (u - 6) // 2
                    dve.wait_ge(o_hi_done, 2 * p + h + 1)
                    v.tensor_tensor(o_lo[:, ds(2 * p + h, 1), :], T0[:, 3 * TS:3 * TS + T],
                                    o_hi[:, ds(2 * p + h, 1), :].bitcast(f32), ALU.subtract).then_inc(o_lo_done, 1)

            v.memset(c_sum[:], 0.0).then_inc(conv_summed, 1)
            dve.wait_ge(pads, 1)
            for u in range(12):
                low_half(W_HEAD, 0, u + 2)
                convolve(0, u)
            with dve.Fori(1, PAIRS) as i:
                step.enter(i, CONV_STEPS + 8, 1)
                for u in range(12):
                    low_half(W_HEAD, i, u + 2)
                    attend(i - 1, u)
                    convolve(i, u)
                step.leave(PAIRS - 1)

            for i0 in (0, 1, 2):
                loop = ExitStack()
                i = (0, None, W_MERGE.loops - 1)[i0] if i0 != 1 else loop.enter_context(
                    dve.Fori(1, W_MERGE.loops - 1))
                for u in range(14):
                    if i0 == 0 and u == 7:
                        attend(PAIRS - 1, 8)
                    low_half(W_MERGE, i, u + 2)
                    if i0 == 0 and u < 6:
                        attend(PAIRS - 1, u)
                    if i0 == 0 and 5 <= u < 7:
                        attend(PAIRS - 1, u + 1)
                    if i0 == 0 and u == 1:
                        dve.wait_ge(mean_done, 1)
                        v.tensor_scalar(ln_rstd[:], M[2][:, 0:T], 1.0 / DC, None, ALU.mult).then_inc(dve_step, 1)
                        dve.wait_ge(dve_step, step.up())
                        for c in range(KC):
                            v.tensor_tensor(c_all[:, c, :], c_all[:, c, :], ln_rstd[:], ALU.subtract)\
                                .then_inc(centred, 1)
                    if i0 == 0 and u == 6:
                        dve.wait_ge(ln_std, 1)
                        v.tensor_scalar(ln_var[:], S0[:, 0:T], 1.0 / DC, EPS, ALU.mult, ALU.add).then_inc(dve_step, 1)
                        step.up()
                        newton(ln_rstd[:], ln_var[:], c_sq[:, 0, :]).then_inc(dve_step, 1)
                        dve.wait_ge(dve_step, step.up())
                    if i0 == 0 and u in (7, 8):
                        for c in range(4 * (u - 7), 4 * (u - 7) + 4):
                            v.tensor_tensor(c_all[:, c, :], c_all[:, c, :], ln_rstd[:], ALU.mult).then_inc(s_scaled, 1)
                    if i0 == 0 and u in S_HI_AT:
                        c = 4 * S_HI_AT.index(u)
                        dve.wait_ge(s_hi_ready, c // 4 + 1)
                        v.tensor_tensor(s_lo[:, c:c + 4, :], c_all[:, c:c + 4, :], s_hi[:, c:c + 4, :].bitcast(f32),
                                        ALU.subtract).then_inc(s_ready, 1)
                    if u == 11:
                        for b in range(2):
                            dve.wait_ge(act_evac, at(ACT_EV, W_MERGE, i, 3 + b))
                            group_tile(W_MERGE, i, 11, 2, b)
                            v.tensor_tensor(m_tmp[:, b, :], M[b][:, 0:T], sig_g[:, b, :], ALU.mult)\
                                .then_inc(dve_evac, 1)
                    if i0 == 2 and u in (10, 11, 12):
                        merged_low(u - 10)
                for b in range(2):
                    group_tile(W_MERGE, i, 13, 3, b)
                    v.tensor_tensor(m_tmp2[:, b, :], M[2 + b][:, 0:T], sig_a[:, b, :], ALU.mult)\
                        .then_inc(dve_evac, 1)
                    dve.wait_ge(dve_evac, at(DVE_EV, W_MERGE, i, 3 + b))
                    v.tensor_tensor(m_all[:, ds(2 * i + b, 1), :], m_tmp[:, b, :], m_tmp2[:, b, :], ALU.add)\
                        .then_inc(m_done, 1)
                loop.close()
            low_half(W_OUT, 0, 2)
            merged_low(3)

            def add_square(k, b):
                dve.wait_ge(x_squared, k + 1)
                dve.wait_ge(ssq_added, k + 2)
                v.tensor_tensor(ssq[:], ssq[:], sq[:, b, :], ALU.add).then_inc(ssq_added, 1)

            def add_to_x(ph, i, u, g, k, bank, b):
                group_tile(ph, i, u, g, b)
                v.tensor_tensor(xT[:, ds(k, 1), :], bank[:, 0:T], xT[:, ds(k, 1), :], ALU.add).then_inc(dve_evac, 1)

            v.memset(ssq[:], 0.0).then_inc(dve_step, 1)
            dve.wait_ge(dve_step, step.up())
            with dve.Fori(0, W_OUT.loops) as i:
                for u in range(8):
                    if u:
                        low_half(W_OUT, i, u + 2)
                    g = u // 4
                    if u % 4 == 3:
                        for b in range(2):
                            add_to_x(W_OUT, i, u, g, 4 * i + (2 * g + b), SET[g][b], b)
                        for b in range(2):
                            if u == 7 and b == 1:
                                low_half(W_OUT, i, 10)
                            k = 4 * i + (2 * g + b)
                            add_square(k, b)
                            dve.wait_ge(h2_hi_ready, k + 1)
                            v.scalar_tensor_tensor(out=o_lo[:, ds(k, 1), :], in0=xT[:, ds(k, 1), :],
                                                   scalar=G_FFN[:, ds(k, 1)], in1=o_hi[:, ds(k, 1), :].bitcast(f32),
                                                   op0=ALU.mult, op1=ALU.subtract).then_inc(h2_ready, 1)

            for up, down, nk, k0 in ((W_UPA, W_DNA, KFA, 0), (W_UPB, W_DNB, KFB, KFA)):
                for i0 in (0, 1):
                    if i0 == 0 and up is W_UPB:
                        continue
                    loop = ExitStack()
                    first = 1 if up is W_UPA else 0
                    i = 0 if i0 == 0 else loop.enter_context(dve.Fori(first, up.loops))
                    if i0:
                        step.enter(i, 2, first)
                    for u in range(8):
                        if i0 or u:
                            low_half(up, i, u + 2)
                        if i0 == 0 and u == 1:
                            dve.wait_ge(norm_std, 2)
                            newton(rstd[:], var[:], sq[:, 0, :]).then_inc(dve_step, 1)
                            dve.wait_ge(dve_step, step.up())
                        if u == 3:
                            for b in range(2):
                                group_tile(up, i, 3, 0, b)
                                v.tensor_tensor(silu_g[:, b, :], M[b][:, 0:T], rstd[:], ALU.mult)\
                                    .then_inc(dve_evac, 1)
                        if u == 5:
                            for b in range(2):
                                dve.wait_ge(silu_done, 2 * i + (k0 + b + 1))
                                v.tensor_tensor(silu_g[:, b, :], silu_g[:, b, :], rstd[:], ALU.mult)\
                                    .then_inc(dve_step, 1)
                                done = step.up()
                            dve.wait_ge(dve_step, done)
                    for b in range(2):
                        group_tile(up, i, 7, 1, b)
                        v.tensor_tensor(act_f[:, b, :], SET[1][b][:, 0:T], silu_g[:, b, :], ALU.mult)\
                            .then_inc(dve_evac, 1)
                    for b in range(2):
                        dve.wait_ge(act_hi_ready, 2 * i + (k0 + b + 1))
                        v.tensor_tensor(act_lo[:, ds(2 * i + b, 1), :], act_f[:, b, :],
                                        act_hi[:, ds(2 * i + b, 1), :].bitcast(f32), ALU.subtract)\
                            .then_inc(act_lo_ready, 1)
                    if i0:
                        step.leave(up.loops - first)
                    loop.close()
                n = nk // KU
                if down is W_DNA:
                    with dve.Fori(0, down.loops) as i:
                        for u in range(n):
                            low_half(down, i, u + 2)
                        for b in range(2):
                            add_to_x(down, i, n - 1, 0, 2 * i + b, (T0, T1)[b], b)

            v.memset(ssq[:], 0.0).then_inc(dve_step, 1)
            dve.wait_ge(dve_step, step.up())
            for i0 in (0, 1, 2):
                loop = ExitStack()
                i = (0, None, W_DNB.loops - 1)[i0] if i0 != 1 else loop.enter_context(dve.Fori(1, W_DNB.loops - 1))
                for u in range(n):
                    if i0 < 2 or u + 2 < n:
                        low_half(W_DNB, i, u + 2)
                for b in range(2):
                    add_to_x(W_DNB, i, n - 1, 0, 2 * i + b, (T0, T1)[b], b)
                for b in range(2):
                    k = 2 * i + b
                    if i0 < 2:
                        add_square(k + KD, b)
                    else:
                        dve.wait_ge(dve_evac, at(DVE_EV, W_DNB, i, b + 1))
                    if i0:
                        dve.wait_ge(y_T, 2 * i + (b - 1))
                    v.tensor_scalar(y_c[:, b, :], xT[:, ds(k, 1), :], G_FIN[:, ds(k, 1)], None, ALU.mult)\
                        .then_inc(y_ready, 1)
                loop.close()
            dve.wait_ge(y_std, 2)
            v.tensor_scalar(stat_v[:, 0:2], T0[:, 0:2], 1.0 / D, EPS, ALU.mult, ALU.add).then_inc(dve_step, 1)
            step.up()
            v.tensor_scalar(stat_v[0:TS, 2:3], T0[0:TS, 2:3], 1.0 / D, EPS, ALU.mult, ALU.add).then_inc(dve_step, 1)
            step.up()
            newton(stat_r[:], stat_v[:], stat_t[:]).then_inc(y_rstd, 1)
            dve.wait_ge(y_rstd, 1)
            dve.wait_ge(y_evac, KD + 2)
            for t, n in ((0, P), (2, TS)):
                for c in HALVES:
                    v.tensor_scalar(y_tok[0:n, t, c], y_tok[0:n, t, c], stat_r[0:n, t:t + 1], None, ALU.mult)\
                        .then_inc(y_scaled, 1)


_INS = ["x_prompt", "x_sample", "cache_conv", "cache_k", "cache_v", "cache_kidx", "g_mix", "w_in", "conv_w",
        "conv_b", "conv_ln_g", "conv_ln_b", "w_conv_out", "idx_ln_g", "idx_ln_b", "w_attn_out", "w_out",
        "g_ffn", "w_gate", "w_up", "w_down", "g_final"]


def kernel(**inputs):
    import numpy as np
    import concourse.bacc as bacc
    from concourse.bass_utils import run_bass_kernel_spmd

    nc = bacc.Bacc("TRN2", target_bir_lowering=False, num_devices=1)
    arrays, a = {}, {}
    for name in _INS:
        x = np.ascontiguousarray(inputs[name])
        arrays[f"in_{name}"] = x
        a[name] = nc.dram_tensor(f"in_{name}", x.shape, mybir.dt.from_np(x.dtype), kind="ExternalInput").ap()
    b, tp, d = inputs["x_prompt"].shape
    ts = inputs["x_sample"].shape[1]
    depth, taps, dc = inputs["conv_w"].shape
    heads, hd = inputs["cache_k"].shape[3:]
    di = inputs["cache_kidx"].shape[3]
    shapes = {"y_prompt": (b, tp, d), "y_sample": (b, ts, d),
              "conv_p": (depth, b, taps - 1, dc), "k_p": (depth, b, tp, heads, hd), "v_p": (depth, b, tp, heads, hd),
              "kidx_p": (depth, b, tp, di),
              "conv_s": (depth, b, taps - 1, dc), "k_s": (depth, b, ts, heads, hd), "v_s": (depth, b, ts, heads, hd),
              "kidx_s": (depth, b, ts, di)}
    o = {n: nc.dram_tensor(f"out_{n}", s, mybir.dt.float32, kind="ExternalOutput").ap() for n, s in shapes.items()}
    chunk_causal_conformer_kernel(nc, a, o)
    r = run_bass_kernel_spmd(nc, [arrays], core_ids=[0])
    return tuple(r.results[0][f"out_{n}"] for n in shapes)
```
